# Optimizing a Trainium2 kernel written in Bass

```python
import math
import jax, jax.numpy as jnp
from jax import lax
import numpy as np

D_MODEL = 1024
BATCH = 1
SEQ = 512
DEPTH = 2

CHUNK = 64
Q_BLOCK = 128
EPS = 1e-6
ROPE_THETA = 10000.0

CONV_DIM = D_MODEL
CONV_W = 3
SSD_HEADS = 16
SSD_HEAD_DIM = 64
SSD_DIM = SSD_HEADS * SSD_HEAD_DIM
SSD_GROUPS = 2
SSD_STATE = 64
SSD_CONV_W = 4
SSD_CONV_DIM = SSD_DIM + 2 * SSD_GROUPS * SSD_STATE
IN_EVEN = 3 * CONV_DIM + SSD_DIM + SSD_CONV_DIM + SSD_HEADS
MIX_EVEN = CONV_DIM + SSD_DIM
DIFF_HEADS = 8
DIFF_HEAD_DIM = 64
D_FF = 2816
N_EXPERTS = 8
TOP_K = 2
MOE_BLOCK = 128
N_EVEN = (DEPTH + 1) // 2
N_ODD = DEPTH // 2

kernel_name = "hybrid_conv_ssd_diffattn_moe_trunk"

def rmsnorm(x, g):
    xf = x.astype(jnp.float32)
    xf = xf * lax.rsqrt(jnp.mean(xf * xf, axis=-1, keepdims=True) + EPS)
    return (xf * g.astype(jnp.float32)).astype(x.dtype)

def causal_dwconv(x, w):
    k, c = w.shape
    return lax.conv_general_dilated(
        x, w.astype(x.dtype)[:, None, :], window_strides=(1,), padding=[(k - 1, 0)],
        dimension_numbers=("NWC", "WIO", "NWC"), feature_group_count=c)

def swiglu(x, w_gate, w_up, w_down):
    return (jax.nn.silu(x @ w_gate) * (x @ w_up)) @ w_down

def ssd_scan(x, dt, a, bm, cm):
    b, s, g, r, p = x.shape
    n = bm.shape[-1]
    nc = s // CHUNK
    x = x.reshape(b, nc, CHUNK, g, r, p)
    dt = dt.reshape(b, nc, CHUNK, g, r)
    bm = bm.reshape(b, nc, CHUNK, g, n)
    cm = cm.reshape(b, nc, CHUNK, g, n)
    xdt = x * dt[..., None]
    a_cs = jnp.cumsum(jnp.moveaxis(dt * a, 2, -1), axis=-1)
    idx = jnp.arange(CHUNK)
    tri = idx[:, None] >= idx[None, :]
    seg = a_cs[..., :, None] - a_cs[..., None, :]
    decay = jnp.exp(jnp.where(tri, seg, -jnp.inf))
    cb = jnp.einsum("bclgn,bcsgn->bcgls", cm, bm)
    y_diag = jnp.einsum("bcgrls,bcsgrp->bclgrp", cb[:, :, :, None] * decay, xdt)
    decay_states = jnp.exp(a_cs[..., -1:] - a_cs)
    xw = xdt * jnp.moveaxis(decay_states, -1, 2)[..., None]
    states = jnp.einsum("bclgn,bclgrp->bcgrpn", bm, xw)
    chunk_decay = jnp.exp(a_cs[..., -1])

    def step(h, inp):
        st, dec = inp
        return h * dec[..., None, None] + st, h

    h0 = jnp.zeros((b, g, r, p, n), x.dtype)
    _, prev = lax.scan(step, h0, (jnp.moveaxis(states, 1, 0), jnp.moveaxis(chunk_decay, 1, 0)))
    prev = jnp.moveaxis(prev, 0, 1)
    y_off = jnp.einsum("bclgn,bcgrpn->bclgrp", cm, prev) * jnp.moveaxis(jnp.exp(a_cs), -1, 2)[..., None]
    return (y_diag + y_off).reshape(b, s, g, r, p)

def conv_ssd_mixer(h, w_in, conv_w, ssd_conv_w, ssd_conv_b, dt_bias, a_log, d_skip, ssd_norm_g, w_out):
    b, s, _ = h.shape
    proj = h @ w_in
    cuts = np.cumsum([CONV_DIM, CONV_DIM, CONV_DIM, SSD_DIM, SSD_CONV_DIM]).tolist()
    bg, cg, hv, z, xbc, dt_raw = jnp.split(proj, cuts, axis=-1)
    y_a = bg * causal_dwconv(cg * hv, conv_w)
    xbc = jax.nn.silu(causal_dwconv(xbc, ssd_conv_w) + ssd_conv_b.astype(xbc.dtype))
    xs, bm, cm = jnp.split(xbc, [SSD_DIM, SSD_DIM + SSD_GROUPS * SSD_STATE], axis=-1)
    r = SSD_HEADS // SSD_GROUPS
    f32 = jnp.float32
    dt = jax.nn.softplus(dt_raw.astype(f32) + dt_bias.astype(f32))
    a = -jnp.exp(a_log.astype(f32))
    xs5 = xs.astype(f32).reshape(b, s, SSD_GROUPS, r, SSD_HEAD_DIM)
    y = ssd_scan(xs5, dt.reshape(b, s, SSD_GROUPS, r), a.reshape(SSD_GROUPS, r),
                 bm.astype(f32).reshape(b, s, SSD_GROUPS, SSD_STATE),
                 cm.astype(f32).reshape(b, s, SSD_GROUPS, SSD_STATE))
    y = y + d_skip.astype(f32).reshape(SSD_GROUPS, r)[:, :, None] * xs5
    y = y.reshape(b, s, SSD_DIM) * jax.nn.silu(z.astype(f32))
    yg = y.reshape(b, s, SSD_GROUPS, SSD_DIM // SSD_GROUPS)
    yg = yg * lax.rsqrt(jnp.mean(yg * yg, axis=-1, keepdims=True) + EPS)
    y_b = (yg.reshape(b, s, SSD_DIM) * ssd_norm_g.astype(f32)).astype(h.dtype)
    return jnp.concatenate([y_a, y_b], axis=-1) @ w_out

def rope_tables(seq):
    inv = 1.0 / (ROPE_THETA ** (jnp.arange(0, DIFF_HEAD_DIM, 2, dtype=jnp.float32) / DIFF_HEAD_DIM))
    ang = jnp.arange(seq, dtype=jnp.float32)[:, None] * inv[None, :]
    return jnp.cos(ang), jnp.sin(ang)

def apply_rope(x, cos, sin):
    xf = x.astype(jnp.float32)
    half = xf.shape[-1] // 2
    x1, x2 = xf[..., :half], xf[..., half:]
    c, s_ = cos[None, :, None, :], sin[None, :, None, :]
    return jnp.concatenate([x1 * c - x2 * s_, x2 * c + x1 * s_], axis=-1).astype(x.dtype)

def diff_attention(h, w_qkv, q_norm, k_norm, lam_q1, lam_k1, lam_q2, lam_k2, sub_norm, w_o, lambda_init, cos, sin):
    b, s, _ = h.shape
    q, k, v = jnp.split(h @ w_qkv, 3, axis=-1)
    q = apply_rope(rmsnorm(q.reshape(b, s, 2 * DIFF_HEADS, DIFF_HEAD_DIM), q_norm), cos, sin)
    k = apply_rope(rmsnorm(k.reshape(b, s, 2 * DIFF_HEADS, DIFF_HEAD_DIM), k_norm), cos, sin)
    v = v.reshape(b, s, DIFF_HEADS, 2 * DIFF_HEAD_DIM)
    q = jnp.transpose(q, (0, 2, 1, 3))
    k = jnp.transpose(k, (0, 2, 1, 3))
    v = jnp.transpose(v, (0, 2, 1, 3))
    f32 = jnp.float32
    lam = (jnp.exp(jnp.sum(lam_q1.astype(f32) * lam_k1.astype(f32)))
           - jnp.exp(jnp.sum(lam_q2.astype(f32) * lam_k2.astype(f32))) + lambda_init)
    scale = 1.0 / math.sqrt(DIFF_HEAD_DIM)
    outs = []
    for q0 in range(0, s, Q_BLOCK):
        q1 = q0 + Q_BLOCK
        qb, kb, vb = q[:, :, q0:q1], k[:, :, :q1], v[:, :, :q1]
        sc = jnp.einsum("bhqd,bhkd->bhqk", qb, kb).astype(f32) * scale
        qpos = jnp.arange(q0, q1)
        kpos = jnp.arange(q1)
        mask = (kpos[None, :] // CHUNK) <= (qpos[:, None] // CHUNK)
        p = jax.nn.softmax(jnp.where(mask, sc, -jnp.inf), axis=-1)
        p = p.reshape(b, DIFF_HEADS, 2, Q_BLOCK, q1)
        a = p[:, :, 0] - lam * p[:, :, 1]
        outs.append(jnp.einsum("bhqk,bhkd->bhqd", a.astype(v.dtype), vb))
    o = jnp.concatenate(outs, axis=2)
    o = rmsnorm(o, sub_norm) * (1.0 - lambda_init)
    o = jnp.transpose(o, (0, 2, 1, 3)).reshape(b, s, DIFF_HEADS * 2 * DIFF_HEAD_DIM)
    return o @ w_o

def moe_swiglu(h, w_router, w_gate_e, w_up_e, w_down_e):
    b, s, d = h.shape
    t = b * s
    xf = h.reshape(t, d)
    logits = (xf @ w_router).astype(jnp.float32)
    top_logit, top_idx = lax.top_k(logits, TOP_K)
    gates = jax.nn.softmax(top_logit, axis=-1)
    flat_e = top_idx.reshape(-1)
    flat_tok = jnp.repeat(jnp.arange(t, dtype=jnp.int32), TOP_K)
    flat_g = gates.reshape(-1)
    order = jnp.argsort(flat_e)
    se, st, sg = flat_e[order], flat_tok[order], flat_g[order]
    counts = jnp.bincount(flat_e, length=N_EXPERTS)
    starts = jnp.cumsum(counts) - counts
    padded = (counts + MOE_BLOCK - 1) // MOE_BLOCK * MOE_BLOCK
    pends = jnp.cumsum(padded)
    pstarts = pends - padded
    n_assign = t * TOP_K
    dest = pstarts[se] + (jnp.arange(n_assign) - starts[se])
    cap = n_assign + N_EXPERTS * MOE_BLOCK
    n_blocks = cap // MOE_BLOCK
    slot_tok = jnp.full((cap,), t, jnp.int32).at[dest].set(st)
    slot_gate = jnp.zeros((cap,), jnp.float32).at[dest].set(sg)
    block_e = jnp.minimum(jnp.searchsorted(pends, jnp.arange(n_blocks) * MOE_BLOCK, side="right"), N_EXPERTS - 1)
    xpad = jnp.concatenate([xf, jnp.zeros((1, d), xf.dtype)], axis=0)
    xb = xpad[slot_tok].reshape(n_blocks, MOE_BLOCK, d)

    def expert_block(args):
        xblk, e = args
        return swiglu(xblk, w_gate_e[e], w_up_e[e], w_down_e[e])

    yb = lax.map(expert_block, (xb, block_e)).reshape(cap, d)
    out = jnp.zeros((t + 1, d), jnp.float32).at[slot_tok].add(yb.astype(jnp.float32) * slot_gate[:, None])
    return out[:t].astype(h.dtype).reshape(b, s, d)

def setup_inputs(seed: int = 0) -> dict:
    key = jax.random.key(seed)
    ks = iter(jax.random.split(key, 48))
    f32 = jnp.float32

    def normal(shape, scale):
        return jax.random.normal(next(ks), shape, f32) * scale

    def gain(shape):
        return 1.0 + normal(shape, 0.02)

    D, F, E = D_MODEL, D_FF, N_EXPERTS
    dt0 = jnp.exp(jax.random.uniform(next(ks), (N_EVEN, SSD_HEADS), f32) * (math.log(0.1) - math.log(0.001)) + math.log(0.001))
    inp = {
        "x": normal((BATCH, SEQ, D), 1.0),
        "even_norm_mix": gain((N_EVEN, D)),
        "even_w_in": normal((N_EVEN, D, IN_EVEN), D ** -0.5),
        "even_conv_w": normal((N_EVEN, CONV_W, CONV_DIM), CONV_W ** -0.5),
        "ssd_conv_w": normal((N_EVEN, SSD_CONV_W, SSD_CONV_DIM), SSD_CONV_W ** -0.5),
        "ssd_conv_b": normal((N_EVEN, SSD_CONV_DIM), 0.02),
        "ssd_dt_bias": dt0 + jnp.log(-jnp.expm1(-dt0)),
        "ssd_a_log": jnp.log(jax.random.uniform(next(ks), (N_EVEN, SSD_HEADS), f32, 1.0, 16.0)),
        "ssd_d": gain((N_EVEN, SSD_HEADS)),
        "ssd_norm_g": gain((N_EVEN, SSD_DIM)),
        "even_w_out": normal((N_EVEN, MIX_EVEN, D), MIX_EVEN ** -0.5),
        "even_norm_ffn": gain((N_EVEN, D)),
        "ffn_w_gate": normal((N_EVEN, D, F), D ** -0.5),
        "ffn_w_up": normal((N_EVEN, D, F), D ** -0.5),
        "ffn_w_down": normal((N_EVEN, F, D), F ** -0.5),
        "odd_norm_mix": gain((N_ODD, D)),
        "attn_w_qkv": normal((N_ODD, D, 3 * D), D ** -0.5),
        "attn_q_norm": gain((N_ODD, DIFF_HEAD_DIM)),
        "attn_k_norm": gain((N_ODD, DIFF_HEAD_DIM)),
        "attn_lambda_q1": normal((N_ODD, DIFF_HEAD_DIM), 0.1),
        "attn_lambda_k1": normal((N_ODD, DIFF_HEAD_DIM), 0.1),
        "attn_lambda_q2": normal((N_ODD, DIFF_HEAD_DIM), 0.1),
        "attn_lambda_k2": normal((N_ODD, DIFF_HEAD_DIM), 0.1),
        "attn_sub_norm": gain((N_ODD, 2 * DIFF_HEAD_DIM)),
        "attn_w_o": normal((N_ODD, D, D), D ** -0.5),
        "odd_norm_ffn": gain((N_ODD, D)),
        "moe_w_router": normal((N_ODD, D, E), D ** -0.5),
        "moe_w_gate": normal((N_ODD, E, D, F), D ** -0.5),
        "moe_w_up": normal((N_ODD, E, D, F), D ** -0.5),
        "moe_w_down": normal((N_ODD, E, F, D), F ** -0.5),
    }
    return inp

def reference(x, even_norm_mix, even_w_in, even_conv_w, ssd_conv_w, ssd_conv_b, ssd_dt_bias, ssd_a_log,
              ssd_d, ssd_norm_g, even_w_out, even_norm_ffn, ffn_w_gate, ffn_w_up, ffn_w_down,
              odd_norm_mix, attn_w_qkv, attn_q_norm, attn_k_norm, attn_lambda_q1, attn_lambda_k1,
              attn_lambda_q2, attn_lambda_k2, attn_sub_norm, attn_w_o, odd_norm_ffn,
              moe_w_router, moe_w_gate, moe_w_up, moe_w_down):
    cos, sin = rope_tables(x.shape[1])
    for layer in range(DEPTH):
        i = layer // 2
        if layer % 2 == 0:
            h = rmsnorm(x, even_norm_mix[i])
            x = x + conv_ssd_mixer(h, even_w_in[i], even_conv_w[i], ssd_conv_w[i], ssd_conv_b[i],
                                   ssd_dt_bias[i], ssd_a_log[i], ssd_d[i], ssd_norm_g[i], even_w_out[i])
            h = rmsnorm(x, even_norm_ffn[i])
            x = x + swiglu(h, ffn_w_gate[i], ffn_w_up[i], ffn_w_down[i])
        else:
            lambda_init = 0.8 - 0.6 * math.exp(-0.3 * layer)
            h = rmsnorm(x, odd_norm_mix[i])
            x = x + diff_attention(h, attn_w_qkv[i], attn_q_norm[i], attn_k_norm[i], attn_lambda_q1[i],
                                   attn_lambda_k1[i], attn_lambda_q2[i], attn_lambda_k2[i], attn_sub_norm[i],
                                   attn_w_o[i], lambda_init, cos, sin)
            h = rmsnorm(x, odd_norm_ffn[i])
            x = x + moe_swiglu(h, moe_w_router[i], moe_w_gate[i], moe_w_up[i], moe_w_down[i])
    return x


_drawn_inputs = setup_inputs


def setup_inputs(seed=0):
    import zlib

    import numpy as np

    out = dict(_drawn_inputs(seed))
    spreads = {}
    factors = {'ssd_norm_g': 2.799,
     'even_norm_ffn': 2.736,
     'attn_q_norm': 3.157,
     'attn_k_norm': 4.298,
     'attn_lambda_q1': 3.038,
     'attn_lambda_k1': 3.929,
     'attn_lambda_k2': 3.842,
     'attn_sub_norm': 21.672,
     'odd_norm_ffn': 8.0}
    for name, (base, spread) in spreads.items():
        noise = np.random.default_rng([zlib.crc32(name.encode()), seed]).standard_normal(out[name].shape)
        drawn = base * np.exp(spread * noise) if base else spread * noise
        out[name] = __import__('jax').numpy.asarray(drawn.astype(out[name].dtype))
    for name, factor in factors.items():
        out[name] = (out[name] * factor).astype(out[name].dtype)
    return out
```

```python
import math

import numpy as np

import concourse.bass as bass
from concourse import mybir

F32 = mybir.dt.float32
F32R = mybir.dt.float32r
I32 = mybir.dt.int32
U32 = mybir.dt.uint32
ALU = mybir.AluOpType
ACT = mybir.ActivationFunctionType
AX = mybir.AxisListType

P = 128
D = 1024
SEQ = 512
NT = SEQ // P
KD = D // P
EPS = 1e-6

SSD_HEADS, SSD_HD, SSD_N = 16, 64, 64
GROUP_HEADS = SSD_HEADS // 2
XBC_TILES = (D + 4 * SSD_N) // P
COL_CG, COL_HV, COL_Z, COL_XBC = D, 2 * D, 3 * D, 4 * D
COL_END = 4 * D + XBC_TILES * P + SSD_HEADS

HEADS, HD = 16, 64
PAIRS = HEADS // 2
SCALE = 1.0 / math.sqrt(HD)
LAMBDA_INIT = 0.8 - 0.6 * math.exp(-0.3)
NEG = -1e30

FF = 2816
FT = FF // P
HALF_FT = FT // 2
HALF_UNITS = (HALF_FT + 1) // 2

E = 8
CAP = 160
MAXPASS = (2 * SEQ + E * (CAP - 1)) // CAP
ROUNDS = FT // 2
WSLOTS = 4

RAW_SLOTS = 4
HL_SLOTS = 4
AHEAD = 3
UNIT = KD * P

U_XBC = 0
U_DT = U_XBC + XBC_TILES
U_Z = U_DT + 1
U_A = U_Z + 8
U_OUT = U_A + 3 * KD
U_FF = U_OUT + 16
FF_HALF = 2 * HALF_FT + 2 * HALF_UNITS
U_QKV = U_FF + 2 * FF_HALF
U_WO = U_QKV + 24
N_UNITS = U_WO + 8

G_Z, G_OUT, G_DOWN, G_QKV, G_WO = 0, 2, 4, 8, 14

R_CONV, R_SCONV, R_SBIAS = 0, 3 * KD, 3 * KD + 4 * XBC_TILES
N_ROWS = R_SBIAS + XBC_TILES


def build_trunk(nc, t, y_dram):
    base = (nc.sbuf_base + 63) // 64 * 64
    top = nc.sbuf_usable_end

    def place(name, shape, dtype, offset):
        n = int(np.prod(shape[1:])) * 4
        assert base + offset + n <= top, (name, base + offset + n - top)
        return nc.alloc_sbuf_tensor_at(name, shape, dtype, offset=base + offset), offset + n

    K4 = 4096
    x_sb, o = place("x_sb", [P, NT, D], F32, 0)
    act_a_hi, o = place("act_a_hi", [P, KD, SEQ], F32R, o)
    act_a_lo, o_b = place("act_a_lo", [P, KD, SEQ], F32R, o)
    act_b_hi, o = place("act_b_hi", [P, KD, SEQ], F32R, o_b)
    act_b_lo, o = place("act_b_lo", [P, KD, SEQ], F32R, o)
    raw, o = place("raw", [P, RAW_SLOTS, UNIT], F32, o)
    w_hi, o = place("w_hi", [P, HL_SLOTS, UNIT], F32R, o)
    w_lo, o = place("w_lo", [P, HL_SLOTS, UNIT], F32R, o)
    gain, o = place("gain", [P, D], F32, o)
    htmp, o = place("htmp", [P, D], F32, o)
    ident, o = place("ident", [P, P], F32, o)
    t_incl, o = place("t_incl", [P, P], F32, o)
    t_gt, o = place("t_gt", [P, P], F32, o)
    ones, o = place("ones", [P, P], F32, o)
    cols, o = place("cols", [P, 80], F32, o)
    small, o = place("small", [P, 64], F32, o)
    stat, o = place("stat", [P, 64], F32, o)
    scratch = o

    xbcT, o = place("xbcT", [P, XBC_TILES, SEQ], F32, scratch)
    zs, o = place("zs", [P, NT, D], F32, o)
    xs, o = place("xs", [P, D], F32, o)
    b_tok, o = place("b_tok", [P, P], F32, o)
    xdt, o = place("xdt", [P, D], F32, o)
    xw, o = place("xw", [P, D], F32, o)
    dtri, o = place("dtri", [P, 4, P], F32, o)
    mix, o = place("mix", [P, SSD_HEADS, P], F32, o)
    cbm, o = place("cbm", [P, 2, P], F32, o)
    state, o = place("state", [P, 512], F32, o)
    es, o = place("es", [P, 48], F32, o)
    dts, o = place("dts", [P, 8, NT * SSD_HEADS], F32, o)
    o_conv = o
    conv_in, o = place("conv_in", [P, 520], F32, o_conv)
    conv_acc, cg_sb = htmp[:, 0:SEQ], htmp[:, SEQ:2 * SEQ]
    o_xs = scratch + XBC_TILES * SEQ * 4 + NT * D * 4
    xbc_in, o2 = place("xbc_in", [P, 2, 516], F32, o_xs)
    xbc_acc, o2 = place("xbc_acc", [P, 2, SEQ], F32, o2)
    dt_rows, o2 = place("dt_rows", [P, SEQ], F32, o2)
    rows_sb, o2 = place("rows_sb", [P, P], F32, o2)
    ff_hi, o = place("ff_hi", [P, HALF_FT, SEQ], F32R, scratch)
    ff_lo, o = place("ff_lo", [P, HALF_FT, SEQ], F32R, o)
    ff_gate, o = place("ff_gate", [P, 2, SEQ], F32, o)
    ff_val, o = place("ff_val", [P, 2, SEQ], F32, o)
    q_tok, o = place("q_tok", [P, NT, D], F32, scratch)
    k_tok, o = place("k_tok", [P, NT, D], F32, o)
    v_tok, o = place("v_tok", [P, NT, D], F32, o)
    trig, o = place("trig", [P, NT, 2, 32], F32, o)
    rot_c, o = place("rot_c", [P, 2, NT, HD], F32, o)
    rot_s, o = place("rot_s", [P, 2, NT, HD], F32, o)
    att_small, o = place("att_small", [P, 8 * HD], F32, o)
    head_ss, o = place("head_ss", [P, 64], F32, o)
    rot_tmp, o = place("rot_tmp", [P, SEQ], F32, o_b)
    rot_sum, o = place("rot_sum", [P, SEQ], F32, o)
    sq_tmp, o = place("sq_tmp", [P, SEQ], F32, o)
    qT, o = place("qT", [P, KD, SEQ], F32, SEQ * NT * 4 * 2)
    kT, o = place("kT", [P, KD, SEQ], F32, o)
    probs, o = place("probs", [P, 2, 2, SEQ], F32, scratch)
    diff, o = place("diff", [P, 2, SEQ], F32, o)
    diffT, o = place("diffT", [P, 2, SEQ], F32, o)
    soft, o3 = place("soft", [P, 2, 8], F32, scratch + 64 * 1024 // 1)
    o_tok, o = place("o_tok", [P, NT, D], F32, scratch + NT * D * 4)

    ps = nc.alloc_psum_tensor("ps", [P, 8, 512], F32)

    def flat(ap):
        return ap.bitcast(F32)

    sems = {}

    def sem(name):
        sems[name] = nc.alloc_semaphore(name)
        return sems[name]

    unit_in = [sem(f"unit_in{i}") for i in range(RAW_SLOTS)]
    hi_done, lo_done, unit_used = sem("hi_done"), sem("lo_done"), sem("unit_used")
    x_in, rows_in, small_in, gain_in = sem("x_in"), sem("rows_in"), sem("small_in"), sem("gain_in")
    att_in = sem("att_in")
    masks_ready, pads_ready = sem("masks_ready"), sem("pads_ready")
    zero_ready, y_zeroed = sem("zero_ready"), sem("y_zeroed")
    rows_turned, cols_ready = sem("rows_turned"), sem("cols_ready")
    sq_done, rms_done, h_ready = sem("sq_done"), sem("rms_done"), sem("h_ready")
    turned, hi_ev, lo_ev = sem("turned"), sem("hi_ev"), sem("lo_ev")
    xbc_evac, xbc_conv, xbc_silu = sem("xbc_evac"), sem("xbc_conv"), sem("xbc_silu")
    dt_evac, dt_turned, dt_abs, dt_exp, dt_ready = (sem("dt_evac"), sem("dt_turned"), sem("dt_abs"),
                                                    sem("dt_exp"), sem("dt_ready"))
    z_evac = sem("z_evac")
    cg_evac, cghv_ready, bg_used, ya_hi, ya_lo = (sem("cg_evac"), sem("cghv_ready"), sem("bg_used"),
                                                  sem("ya_hi"), sem("ya_lo"))
    xs_turned, ssd_small, seg_done = sem("xs_turned"), sem("ssd_small"), sem("seg_done")
    xs_evac, es_ready, seg_exp = sem("xs_evac"), sem("es_ready"), sem("seg_exp")
    dtri_ready, xdt_ready, xw_ready = sem("dtri_ready"), sem("xdt_ready"), sem("xw_ready")
    mix_ready, ssd_out, state_ready = sem("mix_ready"), sem("ssd_out"), sem("state_ready")
    dx_ready, y_evac, y_sq, y_rms = sem("dx_ready"), sem("y_evac"), sem("y_sq"), sem("y_rms")
    acc_evac, v_evac = sem("acc_evac"), sem("v_evac")
    ff_silu, ff_mul, ff_hi_done, ff_lo_done = sem("ff_silu"), sem("ff_mul"), sem("ff_hi_done"), sem("ff_lo_done")
    lam_exp, rot_tables, qk_sq, qk_rms, qk_ready = (sem("lam_exp"), sem("rot_tables"), sem("qk_sq"),
                                                    sem("qk_rms"), sem("qk_ready"))
    qk_root = sem("qk_root")
    qk_turned, qk_evac = sem("qk_turned"), sem("qk_evac")
    scores_done, bias_ready, exp_done, diff_ready = (sem("scores_done"), sem("bias_ready"),
                                                     sem("exp_done"), sem("diff_ready"))
    diff_turned, diffT_ready, heads_out, heads_evac = (sem("diff_turned"), sem("diffT_ready"),
                                                       sem("heads_out"), sem("heads_evac"))
    o_sq, o_rms = sem("o_sq"), sem("o_rms")

    def feature_unit(w, c):
        return w[:, c:c + P].rearrange("(k p) n -> p k n", p=P), (KD, P)

    def token_unit(w, k0, c, n=2):
        return w[k0 * P:(k0 + n) * P, c:c + 512].rearrange("(k p) n -> p k n", p=P), (n, 512)

    w_in, w_out = t["even_w_in"][0], t["even_w_out"][0]
    w_gate, w_up, w_down = t["ffn_w_gate"][0], t["ffn_w_up"][0], t["ffn_w_down"][0]
    w_qkv, w_o = t["attn_w_qkv"][0], t["attn_w_o"][0]
    units = [feature_unit(w_in, COL_XBC + P * f) for f in range(XBC_TILES)]
    units += [feature_unit(w_in, COL_END - P)]
    units += [token_unit(w_in, 2 * k, COL_Z + 512 * g) for g in range(2) for k in range(4)]
    units += [feature_unit(w_in, c + P * a) for a in range(KD) for c in (COL_CG, COL_HV, 0)]
    units += [token_unit(w_out, 2 * k, 512 * g) for g in range(2) for k in range(8)]
    for half in range(2):
        units += [feature_unit(w, P * f) for f in range(half * HALF_FT, (half + 1) * HALF_FT)
                  for w in (w_gate, w_up)]
        units += [token_unit(w_down, half * HALF_FT + 2 * k, 512 * g, min(2, HALF_FT - 2 * k))
                  for g in range(2) for k in range(HALF_UNITS)]
    units += [token_unit(w_qkv, 2 * k, 512 * g) for g in range(6) for k in range(4)]
    units += [token_unit(w_o, 2 * k, 512 * g) for g in range(2) for k in range(4)]
    assert len(units) == N_UNITS

    def size(u):
        return units[u][1][0] * units[u][1][1]

    gains = [t["even_norm_mix"], t["ssd_norm_g"], t["even_norm_ffn"], t["odd_norm_mix"]]

    block = nc.Block()
    block.__enter__()

    @block.sync
    def _(sp):
        rows = [(t["even_conv_w"][0].rearrange("j (f p) -> (j f) p", p=P), R_CONV, 3 * KD),
                (t["ssd_conv_w"][0].rearrange("j (f p) -> (j f) p", p=P), R_SCONV, 4 * XBC_TILES),
                (t["ssd_conv_b"].rearrange("o (f p) -> (o f) p", p=P), R_SBIAS, XBC_TILES)]
        sp.dma_start(x_sb[:], t["x"][0].rearrange("(t p) d -> p t d", p=P)).then_inc(x_in, 16)
        sp.dma_start(gain[:], gains[0][0].partition_broadcast(P)).then_inc(gain_in, 16)
        for src, r, n in rows:
            sp.dma_start(rows_sb[r:r + n, :], src).then_inc(rows_in, 16)
        for i, name in enumerate(("ssd_dt_bias", "ssd_a_log", "ssd_d")):
            sp.dma_start(small[:, 16 * i:16 * i + 16], t[name][0].partition_broadcast(P)).then_inc(small_in, 16)

        def load(u):
            src, (k, n) = units[u]
            if u >= RAW_SLOTS:
                sp.wait_ge(lo_done, u - RAW_SLOTS + 1)
            sp.dma_start(raw[:, u % RAW_SLOTS, 0:k * n].rearrange("p (k n) -> p k n", k=k),
                         src).then_inc(unit_in[u % RAW_SLOTS], 16)

        def load_gain(k):
            sp.wait_ge(h_ready, NT * k)
            sp.dma_start(gain[:], gains[k][0].partition_broadcast(P)).then_inc(gain_in, 16)

        for u in range(N_UNITS):
            load(u)
            if u == U_XBC + 6:
                sp.wait_ge(zero_ready, 1)
                for r in range(0, y_dram.shape[0], P):
                    m = min(P, y_dram.shape[0] - r)
                    sp.dma_start(y_dram[r:r + m, :], mix[0:m, 0:D // P, :].rearrange("p a b -> p (a b)")
                                 ).then_inc(y_zeroed, 16)
            if u == U_A:
                load_gain(1)
            if u == U_OUT + 8:
                load_gain(2)
            if u == U_FF + 8:
                load_gain(3)
            if u == U_FF + 2 * FF_HALF - 6:
                sp.wait_ge(ff_lo_done, FT)
                sp.dma_start(trig[:], t["rope"].rearrange("(t p) a c -> p t a c", p=P)).then_inc(att_in, 16)
                for i, name in enumerate(("attn_q_norm", "attn_k_norm", "attn_lambda_q1", "attn_lambda_k1",
                                          "attn_lambda_q2", "attn_lambda_k2")):
                    sp.dma_start(att_small[:, HD * i:HD * i + HD],
                                 t[name][0].partition_broadcast(P)).then_inc(att_in, 16)
                sp.dma_start(att_small[:, 6 * HD:8 * HD],
                             t["attn_sub_norm"][0].partition_broadcast(P)).then_inc(att_in, 16)

    @block.tensor
    def _(pe):
        def begin_unit(u):
            pe.wait_ge(lo_done, u + 1)

        def feature_out(u, bank, xh, xl):
            begin_unit(u)
            s = u % HL_SLOTS
            for k in range(KD):
                wh, wl = w_hi[:, s, k * P:(k + 1) * P], w_lo[:, s, k * P:(k + 1) * P]
                pe.matmul(ps[:, bank, :], wh, xh[:, k, :], start=(k == 0), stop=False)
                pe.matmul(ps[:, bank, :], wh, xl[:, k, :], start=False, stop=False)
                last = pe.matmul(ps[:, bank, :], wl, xh[:, k, :], start=False, stop=(k == KD - 1))
            last.then_inc(unit_used, 1)

        def token_out(g, u0, depth, source):
            b0 = 4 * (g % 2)
            for i in range((depth + 1) // 2):
                begin_unit(u0 + i)
                s = (u0 + i) % HL_SLOTS
                for tt in range(NT):
                    for k in range(2 * i, min(2 * i + 2, depth)):
                        xh, xl = source(k, tt)
                        c = (k - 2 * i) * 512
                        wh, wl = w_hi[:, s, c:c + 512], w_lo[:, s, c:c + 512]
                        pe.matmul(ps[:, b0 + tt, :], xh, wh, start=(k == 0), stop=False)
                        pe.matmul(ps[:, b0 + tt, :], xh, wl, start=False, stop=False)
                        last = pe.matmul(ps[:, b0 + tt, :], xl, wh, start=False, stop=(k == depth - 1))
                last.then_inc(unit_used, 1)

        def of(hi, lo, k0=0):
            return lambda k, tt: (hi[:, k - k0, tt * P:(tt + 1) * P], lo[:, k - k0, tt * P:(tt + 1) * P])

        def turn(n, source, first_bank):
            for tt in range(NT):
                pe.wait_ge(h_ready, NT * n + tt + 1)
                for half in range(2):
                    i = 8 * n + 2 * tt + half
                    bank = first_bank + (2 * tt + half) % 4
                    if 2 * tt + half >= 4:
                        pe.wait_ge(lo_ev, i - 3)
                    for j in range(4):
                        c = (4 * half + j) * P
                        mm = pe.transpose(ps[:, bank, j * P:(j + 1) * P], source(tt)[:, c:c + P], ident[:])
                    mm.then_inc(turned, 1)

        pe.wait_ge(masks_ready, 1)
        pe.wait_ge(rows_in, 48)
        pe.transpose(ps[:, 5, 0:N_ROWS], rows_sb[0:N_ROWS, :], ident[0:N_ROWS, 0:N_ROWS]).then_inc(rows_turned, 1)

        turn(0, lambda tt: htmp, 0)
        pe.wait_ge(lo_ev, 8)
        for f in range(XBC_TILES):
            if f >= 4:
                pe.wait_ge(xbc_evac, f - 3)
            feature_out(U_XBC + f, f % 4, act_a_hi, act_a_lo)
        feature_out(U_DT, 4, act_a_hi, act_a_lo)
        pe.wait_ge(dt_evac, 1)
        for tt in range(NT):
            mm = pe.transpose(ps[:, 5, tt * P:(tt + 1) * P], dt_rows[:, tt * P:(tt + 1) * P], ident[:])
        mm.then_inc(dt_turned, 1)
        pe.wait_ge(xbc_evac, XBC_TILES)
        token_out(G_Z, U_Z, KD, of(act_a_hi, act_a_lo))
        pe.wait_ge(dt_abs, 1)
        token_out(G_Z + 1, U_Z + 4, KD, of(act_a_hi, act_a_lo))

        def ssd_first(c):
            ts = slice(c * P, (c + 1) * P)
            if c >= 1:
                pe.wait_ge(y_evac, c)
                pe.wait_ge(state_ready, c)
            else:
                pe.wait_ge(xbc_silu, XBC_TILES)
                pe.wait_ge(z_evac, 2 * NT)
                pe.wait_ge(dt_ready, 1)
            for f in range(KD):
                pe.transpose(ps[:, 3 + f // 4, (f % 4) * P:(f % 4 + 1) * P], xbcT[:, f, ts], ident[:])
            pe.transpose(ps[:, 5, 0:P], xbcT[:, KD, ts], ident[:]).then_inc(xs_turned, 1)
            d = dts[:, 1, c * 16:c * 16 + 16]
            pe.matmul(ps[:, 5, 128:144], t_incl[:], d, start=True, stop=True)
            pe.matmul(ps[:, 5, 144:160], t_gt[:], d, start=True, stop=True)
            pe.matmul(ps[:, 5, 160:176], ones[:], d, start=True, stop=True)
            for g in range(2):
                r = slice(64 * g, 64 * g + 64)
                pe.drain()
                mm = pe.matmul(ps[:, 5, 192 + P * g:192 + P * g + P], xbcT[r, KD, ts], xbcT[r, KD + 1, ts],
                               start=True, stop=True)
            mm.then_inc(ssd_small, 1)
            for h in range(4):
                pe.wait_ge(dtri_ready, 4 * c + h + 1)
                if h >= 2:
                    pe.wait_ge(seg_exp, 4 * c + h - 1)
                pe.matmul(ps[:, 6 + h % 2, :], t_gt[:], dtri[:].rearrange("p a b -> p (a b)"),
                          start=True, stop=True).then_inc(seg_done, 1)

        def ssd_second(c):
            ts = slice(c * P, (c + 1) * P)
            pe.wait_ge(mix_ready, 4 * (c + 1))
            pe.wait_ge(xdt_ready, c + 1)
            pe.wait_ge(xw_ready, c + 1)
            pe.wait_ge(xs_evac, c + 1)
            for h in range(SSD_HEADS):
                q = h * SSD_HD
                pe.matmul(ps[:, 3 + h // 8, q % 512:q % 512 + SSD_HD], mix[:, h, :], xdt[:, q:q + SSD_HD],
                          start=True, stop=True)
            if c >= 1:
                for g in range(2):
                    r = slice(64 * g, 64 * g + 64)
                    mm = pe.matmul(ps[:, 6 + g, :], xbcT[r, KD + 1, ts], state[r, :], start=True, stop=True)
            if c < NT - 1:
                pe.wait_ge(es_ready, c + 1)
                for g in range(2):
                    r = slice(64 * g, 64 * g + 64)
                    mm = pe.matmul(ps[r, 5, :], b_tok[:, r], xw[:, 512 * g:512 * g + 512], start=True, stop=True)
            mm.then_inc(ssd_out, 1)

        for a in range(KD):
            if a == 0:
                pe.wait_ge(z_evac, 2 * NT)
            else:
                pe.wait_ge(cg_evac, a)
            feature_out(U_A + 3 * a, 0, act_a_hi, act_a_lo)
            if a >= 1:
                pe.wait_ge(cghv_ready, a)
            feature_out(U_A + 3 * a + 1, 1, act_a_hi, act_a_lo)
            if a >= 1:
                pe.wait_ge(bg_used, a)
            feature_out(U_A + 3 * a + 2, 2, act_a_hi, act_a_lo)
            (ssd_second if a % 2 else ssd_first)(a // 2)

        pe.wait_ge(bg_used, KD)
        pe.wait_ge(y_evac, NT)
        turn(1, lambda tt: zs[:, tt, :], 0)
        pe.wait_ge(ya_lo, KD)
        pe.wait_ge(lo_ev, 16)

        def mixed(k, tt):
            return of(act_b_hi, act_b_lo)(k, tt) if k < KD else of(act_a_hi, act_a_lo, KD)(k, tt)

        token_out(G_OUT, U_OUT, 2 * KD, mixed)
        token_out(G_OUT + 1, U_OUT + 8, 2 * KD, mixed)

        pe.wait_ge(acc_evac, 8)
        turn(2, lambda tt: htmp, 0)
        pe.wait_ge(lo_ev, 24)
        for half in range(2):
            u0 = U_FF + half * FF_HALF
            if half:
                pe.wait_ge(acc_evac, 12)
            for f in range(HALF_FT):
                n = half * HALF_FT + f
                if n >= 2:
                    pe.wait_ge(ff_mul, n - 1)
                feature_out(u0 + 2 * f, 2 * (n % 2), act_a_hi, act_a_lo)
                feature_out(u0 + 2 * f + 1, 2 * (n % 2) + 1, act_a_hi, act_a_lo)
            pe.wait_ge(ff_lo_done, HALF_FT * (half + 1))
            token_out(G_DOWN + 2 * half, u0 + 2 * HALF_FT, HALF_FT, of(ff_hi, ff_lo))
            if half:
                pe.wait_ge(acc_evac, 16)
            token_out(G_DOWN + 2 * half + 1, u0 + 2 * HALF_FT + HALF_UNITS, HALF_FT, of(ff_hi, ff_lo))

        pe.wait_ge(acc_evac, 24)
        turn(3, lambda tt: htmp, 0)
        pe.wait_ge(lo_ev, 32)
        for g in range(6):
            if g >= 2:
                pe.wait_ge(acc_evac, 24 + 4 * (g - 1))
            token_out(G_QKV + g, U_QKV + 4 * g, KD, of(act_a_hi, act_a_lo))
        pe.wait_ge(qk_ready, 16)
        pe.wait_ge(acc_evac, 40)
        pe.wait_ge(v_evac, 8)
        for i, source in enumerate((q_tok, k_tok)):
            for pair in range(PAIRS):
                n = 8 * i + pair
                if n >= 4:
                    pe.wait_ge(qk_evac, n - 3)
                for tt in range(NT):
                    mm = pe.transpose(ps[:, n % 4, tt * P:(tt + 1) * P],
                                      source[:, tt, pair * P:(pair + 1) * P], ident[:])
                mm.then_inc(qk_turned, 1)
        pe.wait_ge(qk_evac, 16)
        items = [(pair, i) for pair in range(PAIRS) for i in range(NT)]
        N = len(items)
        for n in range(N + 2):
            if n < N:
                pair, i = items[n]
                w = P * (i + 1)
                if n >= 2:
                    pe.wait_ge(exp_done, 2 * (n - 1))
                for m in range(2):
                    r = slice(64 * m, 64 * m + 64)
                    b = 2 * (n % 2) + m
                    pe.matmul(ps[:, b, 0:w], qT[r, pair, i * P:(i + 1) * P], kT[r, pair, 0:w],
                              start=True, stop=False, skip_group_check=True)
                    mm = pe.matmul(ps[:, b, w - 64:w], att_small[r, 0:P], att_small[r, P:P + 64],
                                   start=False, stop=True, skip_group_check=True)
                mm.then_inc(scores_done, 1)
            if 1 <= n <= N:
                pair, i = items[n - 1]
                pe.wait_ge(diff_ready, n)
                if n >= 3:
                    pe.wait_ge(diffT_ready, n - 2)
                for b in range(i + 1):
                    mm = pe.transpose(ps[:, 4 + (n - 1) % 2, b * P:(b + 1) * P],
                                      diff[:, (n - 1) % 2, b * P:(b + 1) * P], ident[:])
                mm.then_inc(diff_turned, 1)
            if n >= 2:
                pair, i = items[n - 2]
                pe.wait_ge(diffT_ready, n - 1)
                if n >= 4:
                    pe.wait_ge(heads_evac, n - 3)
                for b in range(i + 1):
                    mm = pe.matmul(ps[:, 6 + n % 2, 0:P], diffT[:, n % 2, b * P:(b + 1) * P],
                                   v_tok[:, b, pair * P:(pair + 1) * P], start=(b == 0), stop=(b == i))
                mm.then_inc(heads_out, 1)
        turn(4, lambda tt: o_tok[:, tt, :], 0)
        pe.wait_ge(lo_ev, 40)
        token_out(G_WO, U_WO, KD, of(act_b_hi, act_b_lo))
        pe.wait_ge(heads_evac, N)
        token_out(G_WO + 1, U_WO + 4, KD, of(act_b_hi, act_b_lo))

    @block.scalar
    def _(act):
        made = [0]

        def high_parts(upto):
            while made[0] <= min(upto, N_UNITS - 1):
                u = made[0]
                act.wait_ge(unit_in[u % RAW_SLOTS], 16 * (u // RAW_SLOTS + 1))
                if u >= HL_SLOTS:
                    act.wait_ge(unit_used, u - HL_SLOTS + 1)
                act.activation(w_hi[:, u % HL_SLOTS, 0:size(u)], raw[:, u % RAW_SLOTS, 0:size(u)],
                               ACT.Copy).then_inc(hi_done, 1)
                made[0] += 1

        def after(u):
            high_parts(u + AHEAD)
            act.wait_ge(unit_used, u + 1)

        def sums_of_squares(k):
            for tt in range(NT):
                act.drain()
                act.activation(squares, x_sb[:, tt, :], ACT.Square,
                               accum_out=stat[:, 8 * k + tt:8 * k + tt + 1])
            act.drain()
            act.activation(stat[:, 8 * k + 4:8 * k + 8], stat[:, 8 * k:8 * k + 4], ACT.Sqrt,
                           scale=1.0 / D, bias=stat[:, 60:61]).then_inc(rms_done, 1)

        def turned_high(n, hi, first_bank):
            for tt in range(NT):
                for half in range(2):
                    i = 8 * n + 2 * tt + half
                    act.wait_ge(turned, i + 1)
                    act.activation(hi[:, 4 * half:4 * half + 4, tt * P:(tt + 1) * P],
                                   ps[:, first_bank + (2 * tt + half) % 4, :].rearrange("p (a b) -> p a b", a=4),
                                   ACT.Copy).then_inc(hi_ev, 1)

        squares = ps[:, 6:8, :].rearrange("p a b -> p (a b)")

        act.wait_ge(x_in, 16)
        act.wait_ge(pads_ready, 1)
        sums_of_squares(0)
        high_parts(AHEAD)
        turned_high(0, act_a_hi, 0)
        for f in range(XBC_TILES + 1):
            if f < XBC_TILES:
                after(U_XBC + f)
                if f >= 2:
                    act.wait_ge(xbc_conv, f - 1)
                act.activation(xbc_in[:, f % 2, 3:515], ps[:, f % 4, :], ACT.Copy).then_inc(xbc_evac, 1)
            if f >= 1:
                act.wait_ge(xbc_conv, f)
                act.activation(xbcT[:, f - 1, :], xbc_acc[:, (f - 1) % 2, :], ACT.Silu).then_inc(xbc_silu, 1)
        after(U_DT)
        act.activation(dt_rows[:], ps[:, 4, :], ACT.Copy).then_inc(dt_evac, 1)
        for g in range(2):
            high_parts(U_Z + 4 * g + AHEAD)
            if g == 0:
                high_parts(U_Z + 4)
            after(U_Z + 4 * g + 3)
            for tt in range(NT):
                act.activation(zs[:, tt, 512 * g:512 * g + 512], ps[:, 4 * g + tt, :], ACT.Silu).then_inc(z_evac, 1)
        act.wait_ge(dt_abs, 1)
        act.activation(dts[:, 3, :], dts[:, 2, :], ACT.Exp, scale=-1.0)
        act.activation(small[:, 48:64], small[:, 16:32], ACT.Exp).then_inc(dt_exp, 1)

        def ssd_first(c):
            act.wait_ge(xs_turned, c + 1)
            if c >= 1:
                act.wait_ge(ssd_out, c)
                act.wait_ge(dx_ready, c)
            act.activation(xs[:, 0:512], ps[:, 3, :], ACT.Copy)
            act.activation(xs[:, 512:1024], ps[:, 4, :], ACT.Copy)
            act.wait_ge(ssd_small, c + 1)
            act.activation(b_tok[:], ps[:, 5, 0:P], ACT.Copy).then_inc(xs_evac, 1)
            if c >= 1:
                act.wait_ge(y_evac, c)
                act.wait_ge(state_ready, c)
            act.activation(es[:], ps[:, 5, 128:176], ACT.Exp).then_inc(es_ready, 1)
            if c == 0:
                act.wait_ge(y_zeroed, 16 * ((y_dram.shape[0] + P - 1) // P))
            for h in range(4):
                act.wait_ge(seg_done, 4 * c + h + 1)
                act.activation(mix[:, 4 * h:4 * h + 4, :], ps[:, 6 + h % 2, :].rearrange("p (a b) -> p a b", a=4),
                               ACT.Exp).then_inc(seg_exp, 1)

        def ssd_second(c):
            act.wait_ge(y_evac, c + 1)
            for g in range(2):
                act.activation(xw[:, 512 * g:512 * g + 512], zs[:, c, 512 * g:512 * g + 512], ACT.Square,
                               accum_out=stat[:, 40 + 2 * c + g:41 + 2 * c + g])
            act.drain().then_inc(y_sq, 1)

        for a in range(KD):
            after(U_A + 3 * a)
            if a >= 1:
                act.wait_ge(cghv_ready, a)
            act.activation(cg_sb, ps[:, 0, :], ACT.Copy).then_inc(cg_evac, 1)
            high_parts(U_A + 3 * a + 1 + AHEAD)
            after(U_A + 3 * a + 2)
            act.wait_ge(bg_used, a + 1)
            act.activation(act_b_hi[:, a, :], conv_acc, ACT.Copy).then_inc(ya_hi, 1)
            (ssd_second if a % 2 else ssd_first)(a // 2)
        act.drain()
        act.activation(stat[:, 48:56], stat[:, 40:48], ACT.Sqrt, scale=2.0 / D,
                       bias=stat[:, 60:61]).then_inc(y_rms, 1)
        turned_high(1, act_a_hi, 0)
        for g in range(2):
            for i in range(8):
                high_parts(U_OUT + 8 * g + i + AHEAD)
        act.wait_ge(acc_evac, 8)
        act.wait_ge(unit_used, U_FF)
        sums_of_squares(1)
        turned_high(2, act_a_hi, 0)
        for half in range(2):
            u0 = U_FF + half * FF_HALF
            for f in range(HALF_FT):
                n = half * HALF_FT + f
                after(u0 + 2 * f)
                if n >= 2:
                    act.wait_ge(ff_mul, n - 1)
                act.activation(ff_gate[:, n % 2, :], ps[:, 2 * (n % 2), :], ACT.Silu).then_inc(ff_silu, 1)
                high_parts(u0 + 2 * f + 1 + AHEAD)
                act.wait_ge(ff_mul, n + 1)
                if half and f == 0:
                    act.wait_ge(unit_used, u0)
                act.activation(ff_hi[:, f, :], ff_val[:, n % 2, :], ACT.Copy).then_inc(ff_hi_done, 1)
            for i in range(2 * HALF_UNITS):
                high_parts(u0 + 2 * HALF_FT + i + AHEAD)
        act.wait_ge(acc_evac, 24)
        sums_of_squares(2)
        turned_high(3, act_a_hi, 0)
        act.wait_ge(lam_exp, 1)
        act.activation(head_ss[:, 34:36], head_ss[:, 32:34], ACT.Exp).then_inc(lam_exp, 1)
        for g in range(6):
            for i in range(4):
                high_parts(U_QKV + 4 * g + i + AHEAD)
            act.wait_ge(unit_used, U_QKV + 4 * g + 4)
            if g < 4:
                for tt in range(NT):
                    n = 4 * g + tt
                    if n >= 1:
                        act.wait_ge(qk_rms, n)
                    act.activation(sq_tmp[:], ps[:, 4 * (g % 2) + tt, :], ACT.Square).then_inc(qk_sq, 1)
                    act.wait_ge(qk_rms, n + 1)
                    act.activation(head_ss[:, 8:16], head_ss[:, 0:8], ACT.Sqrt, scale=1.0 / HD,
                                   bias=stat[:, 60:61]).then_inc(qk_root, 1)
            else:
                for tt in range(NT):
                    act.activation(v_tok[:, tt, 512 * (g - 4):512 * (g - 4) + 512], ps[:, 4 * (g % 2) + tt, :],
                                   ACT.Copy).then_inc(v_evac, 1)
        for n in range(16):
            act.wait_ge(qk_turned, n + 1)
            act.activation((qT, kT)[n // 8][:, n % 8, :], ps[:, n % 4, :], ACT.Copy).then_inc(qk_evac, 1)
        items = [(pair, i) for pair in range(PAIRS) for i in range(NT)]
        N = len(items)
        for n in range(N + 1):
            if n < N:
                pair, i = items[n]
                w = P * (i + 1)
                act.wait_ge(bias_ready, n + 1)
                if n >= 2:
                    act.wait_ge(diff_ready, n - 1)
                for m in range(2):
                    act.activation(probs[:, n % 2, m, 0:w], ps[:, 2 * (n % 2) + m, 0:w], ACT.Exp, scale=SCALE,
                                   bias=soft[:, n % 2, m:m + 1], accum_out=soft[:, n % 2, 2 + m:3 + m])
                    act.drain().then_inc(exp_done, 1)
            if n >= 1:
                pair, i = items[n - 1]
                w = P * (i + 1)
                act.wait_ge(diff_turned, n)
                if n >= 3:
                    act.wait_ge(heads_out, n - 2)
                act.activation(diffT[:, (n - 1) % 2, 0:w], ps[:, 4 + (n - 1) % 2, 0:w],
                               ACT.Copy).then_inc(diffT_ready, 1)
        act.wait_ge(heads_evac, N)
        act.wait_ge(o_sq, 1)
        act.activation(head_ss[:, 32:64], head_ss[:, 0:32], ACT.Sqrt, scale=1.0 / P,
                       bias=stat[:, 60:61]).then_inc(o_rms, 1)
        turned_high(4, act_b_hi, 0)
        for i in range(8):
            high_parts(U_WO + i + AHEAD)

    @block.gpsimd
    def _(pool):
        made = [0]

        def low_parts(upto):
            while made[0] <= min(upto, N_UNITS - 1):
                u = made[0]
                pool.wait_ge(hi_done, u + 1)
                pool.tensor_tensor(w_lo[:, u % HL_SLOTS, 0:size(u)], raw[:, u % RAW_SLOTS, 0:size(u)],
                                   flat(w_hi[:, u % HL_SLOTS, 0:size(u)]), ALU.subtract).then_inc(lo_done, 1)
                made[0] += 1

        pool.memset(ones[:], 1.0)
        pool.memset(ident[:], 0.0)
        pool.drain()
        pool.affine_select(ident[:], ident[:], [[-1, P]], ALU.not_equal, 1.0, base=0, channel_multiplier=1)
        pool.affine_select(t_incl[:], ones[:], [[1, P]], ALU.is_ge, 0.0, base=0, channel_multiplier=-1)
        pool.affine_select(t_gt[:], ones[:], [[-1, P]], ALU.is_gt, 0.0, base=0, channel_multiplier=1)
        pool.drain().then_inc(masks_ready, 1)
        pool.memset(mix[:, 0:D // P, :], 0.0)
        pool.drain().then_inc(zero_ready, 1)
        low_parts(U_A + AHEAD - 1)

        def heads(ap, lo, n):
            return ap[:, lo:lo + n].unsqueeze(2).to_broadcast([P, n, SSD_HD])

        def ssd_first(c):
            d = dts[:, 1, c * 16:c * 16 + 16]
            for h in range(4):
                if 4 * c + h >= 1:
                    pool.wait_ge(seg_done, 4 * c + h)
                pool.tensor_tensor(dtri[:], t_incl[:].unsqueeze(1).to_broadcast([P, 4, P]),
                                   d[:, 4 * h:4 * h + 4].unsqueeze(2).to_broadcast([P, 4, P]),
                                   ALU.mult).then_inc(dtri_ready, 1)
            pool.wait_ge(xs_evac, c + 1)
            if c >= 1:
                pool.wait_ge(y_evac, c)
                pool.wait_ge(y_sq, c)
            v = xs[:].rearrange("p (h d) -> p h d", h=SSD_HEADS)
            pool.tensor_tensor(xdt[:].rearrange("p (h d) -> p h d", h=SSD_HEADS), v,
                               heads(dts[:, 0], c * 16, 16), ALU.mult).then_inc(xdt_ready, 1)
            pool.wait_ge(es_ready, c + 1)
            pool.drain()
            pool.tensor_tensor(xw[:].rearrange("p (h d) -> p h d", h=SSD_HEADS),
                               xdt[:].rearrange("p (h d) -> p h d", h=SSD_HEADS),
                               heads(es, 16, 16), ALU.mult).then_inc(xw_ready, 1)

        def ssd_second(c):
            pool.wait_ge(ssd_out, c + 1)
            pool.tensor_tensor(xw[:].rearrange("p (h d) -> p h d", h=SSD_HEADS),
                               xs[:].rearrange("p (h d) -> p h d", h=SSD_HEADS),
                               heads(small, 32, 16), ALU.mult).then_inc(dx_ready, 1)

        pool.wait_ge(small_in, 48)
        pool.wait_ge(dt_ready, 1)
        for a in range(KD):
            low_parts(U_A + 3 * a + 2 + AHEAD)
            pool.wait_ge(ya_hi, a + 1)
            pool.tensor_tensor(act_b_lo[:, a, :], conv_acc, flat(act_b_hi[:, a, :]),
                               ALU.subtract).then_inc(ya_lo, 1)
            (ssd_second if a % 2 else ssd_first)(a // 2)
        low_parts(U_FF + AHEAD - 1)
        for half in range(2):
            u0 = U_FF + half * FF_HALF
            for f in range(HALF_FT):
                n = half * HALF_FT + f
                low_parts(u0 + 2 * f + 1 + AHEAD)
                pool.wait_ge(ff_hi_done, n + 1)
                pool.tensor_tensor(ff_lo[:, f, :], ff_val[:, n % 2, :], flat(ff_hi[:, f, :]),
                                   ALU.subtract).then_inc(ff_lo_done, 1)
            low_parts(u0 + FF_HALF - 1 + AHEAD)
        low_parts(N_UNITS - 1)

    @block.vector
    def _(dve):
        def norm(k):
            dve.wait_ge(rms_done, (0, 1, 2)[k] + 1)
            n = (0, 2, 3)[k]
            dve.reciprocal(stat[:, 8 * k + 4:8 * k + 8], stat[:, 8 * k + 4:8 * k + 8])
            dve.drain()
            dve.wait_ge(gain_in, 16 * (n + 1))
            for tt in range(NT):
                if tt >= 1:
                    dve.wait_ge(turned, 8 * n + 2 * tt)
                dve.scalar_tensor_tensor(htmp[:], x_sb[:, tt, :], stat[:, 8 * k + 4 + tt:8 * k + 5 + tt],
                                         gain[:], ALU.mult, ALU.mult).then_inc(h_ready, 1)
                if tt >= 1:
                    turned_low(n, tt - 1, act_a_hi, act_a_lo)
            turned_low(n, NT - 1, act_a_hi, act_a_lo)

        def turned_low(n, tt, hi, lo):
            for half in range(2):
                dve.wait_ge(hi_ev, 8 * n + 2 * tt + half + 1)
                dve.tensor_tensor(lo[:, 4 * half:4 * half + 4, tt * P:(tt + 1) * P],
                                  ps[:, (2 * tt + half) % 4, :].rearrange("p (a b) -> p a b", a=4),
                                  flat(hi[:, 4 * half:4 * half + 4, tt * P:(tt + 1) * P]),
                                  ALU.subtract).then_inc(lo_ev, 1)

        def col(r):
            return cols[:, r:r + 1]

        def add_to_x(g, last_unit, c0):
            dve.wait_ge(unit_used, last_unit + 1)
            for tt in range(NT):
                xx = x_sb[:, tt, c0:c0 + 512]
                dve.tensor_tensor(xx, ps[:, 4 * (g % 2) + tt, :], xx, ALU.add).then_inc(acc_evac, 1)

        dve.memset(stat[:, 60:61], EPS)
        dve.memset(xbc_in[:, :, 0:3], 0.0)
        dve.memset(conv_in[:, 0:2], 0.0)
        dve.drain().then_inc(pads_ready, 1)
        dve.wait_ge(rows_turned, 1)
        dve.tensor_copy(cols[:, 0:N_ROWS], ps[:, 5, 0:N_ROWS])
        norm(0)
        for f in range(XBC_TILES):
            w = [col(R_SCONV + XBC_TILES * j + f) for j in range(4)]
            src, acc = xbc_in[:, f % 2, :], xbc_acc[:, f % 2, :]
            dve.wait_ge(xbc_evac, f + 1)
            if f >= 2:
                dve.wait_ge(xbc_silu, f - 1)
            dve.tensor_scalar(acc, src[:, 0:512], w[0], col(R_SBIAS + f), ALU.mult, ALU.add)
            for j in range(1, 4):
                dve.drain()
                ins = dve.scalar_tensor_tensor(acc, src[:, j:j + 512], w[j], acc, ALU.mult, ALU.add)
            ins.then_inc(xbc_conv, 1)
        T16 = NT * SSD_HEADS
        dve.wait_ge(dt_turned, 1)
        dve.wait_ge(small_in, 48)
        v3 = dts[:, 0, :].rearrange("p (t h) -> p t h", t=NT)
        dve.tensor_tensor(v3, ps[:, 5, :].rearrange("p (t c) -> p t c", t=NT)[:, :, P - 16:P],
                          small[:, 0:16].unsqueeze(1).to_broadcast([P, NT, 16]), ALU.add)
        dve.drain()
        dve.scalar_tensor_tensor(dts[:, 2, :], dts[:, 0, :], -1.0, dts[:, 0, :], ALU.mult,
                                 ALU.max).then_inc(dt_abs, 1)
        dve.wait_ge(dt_exp, 1)
        u, r, q, s = dts[:, 3, :], dts[:, 4, :], dts[:, 5, :], dts[:, 6, :]
        dve.tensor_scalar(r, u, 2.0, None, ALU.add)
        dve.drain()
        dve.reciprocal(r, r)
        dve.drain()
        dve.tensor_tensor(r, r, u, ALU.mult)
        dve.drain()
        dve.tensor_tensor(q, r, r, ALU.mult)
        dve.drain()
        dve.tensor_scalar(s, q, 1.0 / 17, None, ALU.mult)
        for m in (15, 13, 11, 9, 7, 5, 3):
            dve.drain()
            dve.scalar_tensor_tensor(s, s, 1.0 / m, q, ALU.add, ALU.mult)
        dve.drain()
        dve.scalar_tensor_tensor(s, s, 1.0, r, ALU.add, ALU.mult)
        dve.drain()
        dve.tensor_scalar(s, s, 2.0, None, ALU.mult)
        dve.drain()
        dve.scalar_tensor_tensor(dts[:, 0, :], dts[:, 0, :], 0.0, s, ALU.max, ALU.add)
        dve.drain()
        dve.scalar_tensor_tensor(dts[:, 1, :].rearrange("p (t h) -> p t h", t=NT), v3, -1.0,
                                 small[:, 48:64].unsqueeze(1).to_broadcast([P, NT, 16]), ALU.mult,
                                 ALU.mult).then_inc(dt_ready, 1)

        def ssd_first(c):
            dve.wait_ge(es_ready, c + 1)
            for g in range(2):
                dve.tensor_tensor(cbm[:, g, :], ps[:, 5, 192 + P * g:192 + P * g + P], t_incl[:], ALU.mult)
            dve.drain()
            for h in range(4):
                dve.wait_ge(seg_exp, 4 * c + h + 1)
                m = mix[:, 4 * h:4 * h + 4, :]
                dve.tensor_tensor(m, m, cbm[:, h // 2, :].unsqueeze(1).to_broadcast([P, 4, P]),
                                  ALU.mult).then_inc(mix_ready, 1)

        def ssd_second(c):
            def grouped(ap):
                return ap.rearrange("p (h d) -> p h d", h=GROUP_HEADS)

            def spread(rows, lo):
                return es[rows, lo:lo + 8].unsqueeze(2).to_broadcast([rows.stop - rows.start, 8, SSD_HD])

            every = slice(0, P)
            dve.wait_ge(ssd_out, c + 1)
            if c >= 1:
                for g in range(2):
                    y = xdt[:, 512 * g:512 * g + 512]
                    dve.tensor_tensor(grouped(y), grouped(ps[:, 6 + g, :]), spread(every, 8 * g), ALU.mult)
            if c < NT - 1:
                if c == 0:
                    dve.tensor_copy(state[:], ps[:, 5, :]).then_inc(state_ready, 1)
                else:
                    for g in range(2):
                        r = slice(64 * g, 64 * g + 64)
                        dve.tensor_tensor(grouped(state[r, :]), grouped(state[r, :]), spread(r, 32 + 8 * g), ALU.mult)
                    dve.drain()
                    dve.tensor_tensor(state[:], ps[:, 5, :], state[:], ALU.add).then_inc(state_ready, 1)
            dve.wait_ge(dx_ready, c + 1)
            for g in range(2):
                dve.tensor_tensor(xw[:, 512 * g:512 * g + 512], ps[:, 3 + g, :], xw[:, 512 * g:512 * g + 512], ALU.add)
            dve.drain()
            if c >= 1:
                dve.tensor_tensor(xw[:], xw[:], xdt[:], ALU.add)
                dve.drain()
            dve.tensor_tensor(zs[:, c, :], zs[:, c, :], xw[:], ALU.mult).then_inc(y_evac, 1)

        for a in range(KD):
            w = [col(R_CONV + KD * j + a) for j in range(3)]
            dve.wait_ge(unit_used, U_A + 3 * a + 2)
            dve.wait_ge(cg_evac, a + 1)
            dve.tensor_tensor(conv_in[:, 2:514], ps[:, 1, :], cg_sb, ALU.mult).then_inc(cghv_ready, 1)
            if a >= 1:
                dve.wait_ge(ya_lo, a)
            dve.drain()
            dve.tensor_scalar(conv_acc, conv_in[:, 0:512], w[0], None, ALU.mult)
            for j in (1, 2):
                dve.drain()
                dve.scalar_tensor_tensor(conv_acc, conv_in[:, j:j + 512], w[j], conv_acc, ALU.mult, ALU.add)
            dve.wait_ge(unit_used, U_A + 3 * a + 3)
            dve.drain()
            dve.tensor_tensor(conv_acc, ps[:, 2, :], conv_acc, ALU.mult).then_inc(bg_used, 1)
            (ssd_second if a % 2 else ssd_first)(a // 2)
        dve.wait_ge(y_rms, 1)
        dve.wait_ge(gain_in, 32)
        dve.reciprocal(stat[:, 48:56], stat[:, 48:56])
        dve.drain()
        for c in range(NT):
            for g in range(2):
                z = zs[:, c, 512 * g:512 * g + 512]
                ins = dve.scalar_tensor_tensor(z, z, stat[:, 48 + 2 * c + g:49 + 2 * c + g],
                                               gain[:, 512 * g:512 * g + 512], ALU.mult, ALU.mult)
            ins.then_inc(h_ready, 1)
            if c >= 1:
                turned_low(1, c - 1, act_a_hi, act_a_lo)
        turned_low(1, NT - 1, act_a_hi, act_a_lo)
        add_to_x(G_OUT, U_OUT + 7, 0)
        add_to_x(G_OUT + 1, U_OUT + 15, 512)
        norm(1)
        for half in range(2):
            u0 = U_FF + half * FF_HALF
            for f in range(HALF_FT):
                n = half * HALF_FT + f
                dve.wait_ge(unit_used, u0 + 2 * f + 2)
                dve.wait_ge(ff_silu, n + 1)
                if n >= 2:
                    dve.wait_ge(ff_lo_done, n - 1)
                dve.tensor_tensor(ff_val[:, n % 2, :], ps[:, 2 * (n % 2) + 1, :], ff_gate[:, n % 2, :],
                                  ALU.mult).then_inc(ff_mul, 1)
            for g in range(2):
                add_to_x(G_DOWN + 2 * half + g, u0 + 2 * HALF_FT + (g + 1) * HALF_UNITS - 1, 512 * g)
        norm(2)
        dve.wait_ge(att_in, 128)
        for i in range(2):
            g1, g2 = att_small[:, HD * i:HD * i + 32], att_small[:, HD * i + 32:HD * i + 64]
            b1, b2 = (g.unsqueeze(1).to_broadcast([P, NT, 32]) for g in (g1, g2))
            cos, sin = trig[:, :, 0, :], trig[:, :, 1, :]
            dve.tensor_tensor(rot_c[:, i, :, 0:32], cos, b1, ALU.mult)
            dve.tensor_tensor(rot_c[:, i, :, 32:64], cos, b2, ALU.mult)
            dve.scalar_tensor_tensor(rot_s[:, i, :, 0:32], sin, -1.0, b2, ALU.mult, ALU.mult)
            dve.tensor_tensor(rot_s[:, i, :, 32:64], sin, b1, ALU.mult)
        for m in range(2):
            a1, a2 = (att_small[:, HD * (2 + 2 * m + j):HD * (3 + 2 * m + j)] for j in (0, 1))
            dve.tensor_tensor(a1, a1, a2, ALU.mult)
            dve.drain()
            dve.reduce_sum(head_ss[:, 32 + m:33 + m], a1, AX.X)
        dve.drain().then_inc(lam_exp, 1)
        dve.wait_ge(lam_exp, 2)
        dve.tensor_tensor(head_ss[:, 36:37], head_ss[:, 35:36], head_ss[:, 34:35], ALU.subtract)
        dve.drain()
        dve.tensor_scalar(stat[:, 61:62], head_ss[:, 36:37], -LAMBDA_INIT, None, ALU.add)
        dve.memset(att_small[:, 0:192], 0.0)
        dve.drain()
        for r in (0, 64):
            dve.memset(att_small[r:r + 1, 0:64], NEG)
            dve.memset(att_small[r:r + 1, 128:192], 1.0)
        for g in range(4):
            dst, i = (q_tok, k_tok)[g // 2], g // 2
            for tt in range(NT):
                n = 4 * g + tt
                bank = ps[:, 4 * (g % 2) + tt, :].rearrange("p (h d) -> p h d", h=8)
                c3 = rot_c[:, i, tt, :].unsqueeze(1).to_broadcast([P, 8, HD])
                s3 = rot_s[:, i, tt, :]
                tmp, tot = (b[:].rearrange("p (h d) -> p h d", h=8) for b in (rot_tmp, rot_sum))
                dve.wait_ge(qk_sq, n + 1)
                dve.reduce_sum(head_ss[:, 0:8], sq_tmp[:].rearrange("p (h d) -> p h d", h=8),
                               AX.X).then_inc(qk_rms, 1)
                dve.tensor_tensor(tot, bank, c3, ALU.mult)
                dve.tensor_tensor(tmp[:, :, 0:32], bank[:, :, 32:64],
                                  s3[:, 0:32].unsqueeze(1).to_broadcast([P, 8, 32]), ALU.mult)
                dve.tensor_tensor(tmp[:, :, 32:64], bank[:, :, 0:32],
                                  s3[:, 32:64].unsqueeze(1).to_broadcast([P, 8, 32]), ALU.mult).then_inc(acc_evac, 1)
                dve.drain()
                dve.tensor_tensor(tot, tot, tmp, ALU.add)
                dve.wait_ge(qk_root, n + 1)
                dve.reciprocal(head_ss[:, 16:24], head_ss[:, 8:16])
                dve.drain()
                dve.tensor_tensor(dst[:, tt, 512 * (g % 2):512 * (g % 2) + 512].rearrange("p (h d) -> p h d", h=8),
                                  tot, head_ss[:, 16:24].unsqueeze(2).to_broadcast([P, 8, HD]),
                                  ALU.mult).then_inc(qk_ready, 1)
                dve.drain()
        items = [(pair, i) for pair in range(PAIRS) for i in range(NT)]
        N = len(items)
        dve.wait_ge(qk_turned, 16)
        for n in range(N + 2):
            if n < N:
                pair, i = items[n]
                w = P * (i + 1)
                s2 = soft[:, n % 2, :]
                dve.wait_ge(scores_done, n + 1)
                for m in range(2):
                    dve.reduce_max(s2[:, 4 + m:5 + m], ps[:, 2 * (n % 2) + m, 0:w], AX.X)
                dve.drain()
                dve.tensor_scalar(s2[:, 0:2], s2[:, 4:6], -SCALE, None, ALU.mult).then_inc(bias_ready, 1)
            if 1 <= n <= N:
                pair, i = items[n - 1]
                w = P * (i + 1)
                b = (n - 1) % 2
                s2 = soft[:, b, :]
                dve.wait_ge(exp_done, 2 * n)
                dve.reciprocal(s2[:, 4:6], s2[:, 2:4])
                dve.drain()
                dve.tensor_scalar(s2[:, 5:6], s2[:, 5:6], stat[:, 61:62], None, ALU.mult)
                if n >= 3:
                    dve.wait_ge(diff_turned, n - 2)
                dve.tensor_scalar(diff[:, b, 0:w], probs[:, b, 0, 0:w], s2[:, 4:5], None, ALU.mult)
                dve.drain()
                dve.scalar_tensor_tensor(diff[:, b, 0:w], probs[:, b, 1, 0:w], s2[:, 5:6], diff[:, b, 0:w],
                                         ALU.mult, ALU.add).then_inc(diff_ready, 1)
            if n >= 2:
                pair, i = items[n - 2]
                dve.wait_ge(heads_out, n - 1)
                dve.tensor_copy(o_tok[:, i, pair * P:(pair + 1) * P], ps[:, 6 + n % 2, 0:P]).then_inc(heads_evac, 1)
        for tt in range(NT):
            dve.drain()
            dve.tensor_tensor(htmp[:], o_tok[:, tt, :], o_tok[:, tt, :], ALU.mult)
            dve.drain()
            dve.reduce_sum(head_ss[:, 8 * tt:8 * tt + 8], htmp[:].rearrange("p (h d) -> p h d", h=8), AX.X)
        dve.drain().then_inc(o_sq, 1)
        dve.wait_ge(o_rms, 1)
        dve.reciprocal(head_ss[:, 32:64], head_ss[:, 32:64])
        dve.tensor_scalar(att_small[:, 6 * HD:8 * HD], att_small[:, 6 * HD:8 * HD], 1.0 - LAMBDA_INIT, None, ALU.mult)
        dve.drain()
        for tt in range(NT):
            v = o_tok[:, tt, :].rearrange("p (h d) -> p h d", h=8)
            dve.tensor_tensor(v, v, head_ss[:, 32 + 8 * tt:40 + 8 * tt].unsqueeze(2).to_broadcast([P, 8, P]), ALU.mult)
            dve.drain()
            dve.tensor_tensor(v, v, att_small[:, 6 * HD:8 * HD].unsqueeze(1).to_broadcast([P, 8, P]),
                              ALU.mult).then_inc(h_ready, 1)
            if tt >= 1:
                turned_low(4, tt - 1, act_b_hi, act_b_lo)
        turned_low(4, NT - 1, act_b_hi, act_b_lo)
        for g in range(2):
            add_to_x(G_WO + g, U_WO + 4 * g + 3, 512 * g)

    block.__exit__(None, None, None)
    return dict(x_sb=x_sb, sem=sem, place=place, ps=ps, acc_evac=acc_evac)


def build_experts(nc, t, out, place, sem, x_sb, ps, y_dram):
    slot_tok = nc.dram_tensor("slot_tok", ((MAXPASS + 1) * CAP, 1), I32, kind="Internal").ap()
    h_dram = nc.dram_tensor("h_rows", (SEQ, D), F32, kind="Internal").ap()
    CAP2 = CAP - P

    w_gate, o = place("w_gate", [P, WSLOTS, KD, 2 * P], F32, NT * D * 4)
    w_up, o = place("w_up", [P, WSLOTS, KD, 2 * P], F32, o)
    w_down, o_ring = place("w_down", [P, WSLOTS, 2, D], F32, o)
    y_got, _ = place("y_got", [P, 2 * NT, D], F32, NT * D * 4)
    xT, o = place("xT", [P, KD, CAP], F32, o_ring)
    xT_next, o = place("xT_next", [P, KD, CAP], F32, o)
    hid, o = place("hid", [P, FT, CAP], F32, o)
    silu_g, o = place("silu_g", [P, 2, CAP], F32, o)
    yT, o = place("yT", [P, KD, CAP], F32, o)
    x_rows, o = place("x_rows", [P, D], F32, o)
    x_rows2, o = place("x_rows2", [P, D], F32, o)
    y_rows, o = place("y_rows_sb", [P, D], F32, o)
    y_rows2, o = place("y_rows2_sb", [P, D], F32, o)
    hT, _ = place("hT", [P, KD, SEQ], F32, o_ring)
    h_tok, o = place("h_tok", [P, 2, D], F32, o)
    gain, o = place("gain_moe", [P, D], F32, o)
    w_router, o = place("w_router", [P, KD, E], F32, o)
    ident, o = place("ident_moe", [P, P], F32, o)
    ones, o = place("ones_moe", [P, P], F32, o)
    t_lt, o = place("t_lt", [P, P], F32, o)
    rt, o = place("rt", [P, 512], F32, o)
    idx, o = place("idx", [P, 32], I32, o)
    top_i, o = place("top_i", [P, NT, 8], U32, o)

    def cut(lo, n):
        return rt[:, lo:lo + n]

    stat, logits, tops = cut(0, 16), cut(16, 32), cut(48, 32)
    chosen, onehot = cut(80, 8), cut(96, 64)
    sel, rank, cnt = cut(160, 32), cut(192, 32), cut(224, 8)
    nb, end, first = cut(232, 8), cut(240, 8), cut(248, 8)
    slot_f, gate, iota_e, iota_w, pass_f = cut(256, 8), cut(264, 8), cut(272, 8), cut(280, 16), cut(296, 16)
    work, gdiff, eps = cut(320, 64), cut(384, 12), cut(400, 1)
    ones8 = cut(408, 8)
    slot_i, slot_y, tok_i, npass_i, pass_i = idx[:, 0:8], idx[:, 8:16], idx[:, 16:20], idx[:, 20:21], None
    idx_a, idx_b = idx[:, 21:22], idx[:, 22:23]
    pass_t, o = place("pass_t", [P, 16], I32, o)
    zero_i, o = place("zero_i", [P, 32], I32, o)

    moe_in, set_up, rms, h_made, h_sent = (sem("moe_in"), sem("set_up"), sem("moe_rms"), sem("h_made"),
                                           [sem("h_sent0"), sem("h_sent1")])
    h_turned, hT_made, routed = sem("h_turned"), sem("hT_made"), sem("routed")
    gate_diff, gate_exp, sel_made, ranked = sem("gate_diff"), sem("gate_exp"), sem("sel_made"), sem("ranked")
    slots_made, passes_made, table_zero, scattered = (sem("slots_made"), sem("passes_made"),
                                                      sem("table_zero"), sem("scattered"))
    idx_in, rows_got = sem("idx_in"), sem("rows_got")
    x_turned, x_copied, xT_made = sem("x_turned"), sem("x_copied"), sem("xT_made")
    w_in = [sem(f"w_in{s}") for s in range(WSLOTS)]
    tile_done, silu_done, hid_made = sem("tile_done"), sem("silu_done"), sem("hid_made")
    down_done, acc_read = sem("down_done"), sem("acc_read")
    y_turned, y_copied, y_stored, y_free = sem("y_turned"), sem("y_copied"), sem("y_stored"), sem("y_free")
    pool_step = sem("pool_step")
    y_back = [sem(f"y_back{i}") for i in range(2 * NT)]
    out_made, out_stored = sem("out_made"), sem("out_stored")

    def uses(s):
        return (ROUNDS - s + WSLOTS - 1) // WSLOTS

    def last_use(s):
        return s + WSLOTS * (uses(s) - 1)

    def n_passes(eng):
        return eng.value_load(npass_i[0:1, :], min_val=(2 * SEQ + CAP - 1) // CAP, max_val=MAXPASS)

    block = nc.Block()
    block.__enter__()

    @block.sync
    def _(sp):
        sp.dma_start(gain[:], t["odd_norm_ffn"][0].partition_broadcast(P)).then_inc(moe_in, 16)
        sp.dma_start(w_router[:], t["moe_w_router"][0].rearrange("(k p) e -> p k e", p=P)).then_inc(moe_in, 16)
        for tt in range(NT):
            sp.wait_ge(h_made, tt + 1)
            sp.dma_start(h_dram[tt * P:(tt + 1) * P, :], h_tok[:, tt % 2, :]).then_inc(h_sent[tt % 2], 16)
        sp.wait_ge(passes_made, 1)
        n = n_passes(sp)
        with sp.Fori(0, MAXPASS) as w:
            with sp.If(w < n):
                e = sp.value_load(pass_t[0:1, bass.ds(w, 1)], min_val=0, max_val=E - 1)
                for r in range(ROUNDS):
                    s = r % WSLOTS
                    free = r - WSLOTS + 1 + ROUNDS if r >= WSLOTS else last_use(s) + 1
                    sp.wait_ge(down_done, w * ROUNDS + free)
                    c = slice(2 * P * r, 2 * P * (r + 1))
                    sp.dma_start(w_gate[:, s], t["moe_w_gate"][0][e, :, c].rearrange("(k p) n -> p k n", p=P)
                                 ).then_inc(w_in[s], 16)
                    sp.dma_start(w_up[:, s], t["moe_w_up"][0][e, :, c].rearrange("(k p) n -> p k n", p=P)
                                 ).then_inc(w_in[s], 16)
                    sp.dma_start(w_down[:, s], t["moe_w_down"][0][e, c, :].rearrange("(k p) n -> p k n", p=P)
                                 ).then_inc(w_in[s], 16)
                    if r == 5:
                        sp.wait_ge(y_copied, 2 * w + 2)
                        sp.dma_start(y_dram[bass.ds(w * CAP, P), :], y_rows[:]).then_inc(y_stored, 16)
                        sp.dma_start(y_dram[bass.ds(w * CAP + P, CAP2), :], y_rows2[0:CAP2, :]).then_inc(y_stored, 16)
                    if r == 9:
                        sp.wait_ge(y_stored, w * 32 + 32)
                        sp.sem_inc(y_free, 1)
        sp.wait_ge(y_copied, 2 * n + 2)
        sp.dma_start(y_dram[bass.ds(n * CAP, P), :], y_rows[:]).then_inc(y_stored, 16)
        sp.dma_start(y_dram[bass.ds(n * CAP + P, CAP2), :], y_rows2[0:CAP2, :]).then_inc(y_stored, 16)
        for tt in range(NT):
            sp.wait_ge(out_made, tt + 1)
            sp.dma_start(out[0, tt * P:(tt + 1) * P, :], x_sb[:, tt, :]).then_inc(out_stored, 16)
        sp.wait_ge(out_stored, 16 * NT)

    @block.tensor
    def _(pe):
        pe.sem_inc(down_done, ROUNDS)
        pe.sem_inc(y_free, 1)
        pe.wait_ge(set_up, 1)
        for tt in range(NT):
            pe.wait_ge(h_made, tt + 1)
            for half in range(2):
                b = (2 * tt + half) % 4
                if 2 * tt + half >= 4:
                    pe.wait_ge(hT_made, 2 * tt + half - 3)
                for j in range(4):
                    c = (4 * half + j) * P
                    mm = pe.transpose(ps[:, b, j * P:(j + 1) * P], h_tok[:, tt % 2, c:c + P], ident[:])
                mm.then_inc(h_turned, 1)
        pe.wait_ge(hT_made, 8)
        pe.wait_ge(moe_in, 32)
        for tt in range(NT):
            for k in range(KD):
                mm = pe.matmul(ps[:, 4, 8 * tt:8 * tt + 8], hT[:, k, tt * P:(tt + 1) * P], w_router[:, k, :],
                               start=(k == 0), stop=(k == KD - 1))
        mm.then_inc(routed, 1)
        pe.wait_ge(sel_made, 1)
        for tt in range(NT):
            for u in range(tt + 1):
                pe.matmul(ps[:, 5, 8 * tt:8 * tt + 8], (t_lt if u == tt else ones)[:], sel[:, 8 * u:8 * u + 8],
                          start=(u == 0), stop=(u == tt))
        for u in range(NT):
            mm = pe.matmul(ps[:, 5, 32:40], ones[:], sel[:, 8 * u:8 * u + 8], start=(u == 0), stop=(u == NT - 1))
        mm.then_inc(ranked, 1)

        def turn_x_main():
            for k in range(KD):
                mm = pe.transpose(ps[:, 6 + k // 4, (k % 4) * P:(k % 4 + 1) * P], x_rows[:, k * P:(k + 1) * P], ident[:])
            mm.then_inc(x_turned, 1)

        def turn_x_rest():
            for k in range(KD):
                mm = pe.transpose(ps[:, 6, k * CAP2:(k + 1) * CAP2], x_rows2[0:CAP2, k * P:(k + 1) * P],
                                  ident[0:CAP2, 0:CAP2])
            mm.then_inc(x_turned, 1)

        def turn_y(lo, n):
            for k in range(KD):
                mm = pe.transpose(ps[0:n, 6 + k // 4, (k % 4) * P:(k % 4 + 1) * P], yT[:, k, lo:lo + n], ident[:])
            mm.then_inc(y_turned, 1)

        pe.wait_ge(rows_got, 32)
        turn_x_main()
        pe.wait_ge(x_copied, 1)
        turn_x_rest()
        n = n_passes(pe)
        with pe.Fori(0, MAXPASS) as w:
            with pe.If(w < n):
                def hidden(f):
                    s = (f // 2) % WSLOTS
                    c = (f % 2) * P
                    b = 3 + f % 3
                    if f % 2 == 0:
                        pe.wait_ge(w_in[s], w * (48 * uses(s)) + 48 * (f // 2 // WSLOTS + 1))
                    pe.wait_ge(hid_made, w * FT + (FT, FT - 2, FT - 1)[f] if f < 3 else w * FT + (FT + f - 2))
                    for i, wt in enumerate((w_gate, w_up)):
                        for k in range(KD):
                            mm = pe.matmul(ps[:, b, i * CAP:(i + 1) * CAP], wt[:, s, k, c:c + P], xT[:, k, :],
                                           start=(k == 0), stop=(k == KD - 1))
                    mm.then_inc(tile_done, 1)

                def down(r):
                    s = r % WSLOTS
                    pe.wait_ge(hid_made, w * FT + (FT + 2 * r + 2))
                    for f in (2 * r, 2 * r + 1):
                        for d in range(KD):
                            mm = pe.matmul(ps[:, d // 3, (d % 3) * CAP:(d % 3 + 1) * CAP],
                                           w_down[:, s, f % 2, d * P:(d + 1) * P], hid[:, f, :],
                                           start=(f == 0 and d % 3 == 0), stop=(f == FT - 1),
                                           skip_group_check=True)
                    mm.then_inc(down_done, 1)

                pe.wait_ge(xT_made, w + 1)
                for r in range(ROUNDS):
                    if r == 7:
                        pe.wait_ge(x_copied, w * 2 + 3)
                    hidden(2 * r)
                    hidden(2 * r + 1)
                    if r == 1:
                        pe.wait_ge(acc_read, w + 1)
                        pe.wait_ge(x_copied, w * 2 + 2)
                        turn_y(0, P)
                    if r == 2:
                        pe.wait_ge(y_copied, w * 2 + 1)
                        turn_y(P, CAP2)
                    if r == 5:
                        pe.wait_ge(y_copied, w * 2 + 2)
                        pe.wait_ge(rows_got, w * 32 + 64)
                        turn_x_main()
                    if r == 7:
                        turn_x_rest()
                    if r >= 1:
                        down(r - 1)
                down(ROUNDS - 1)
        pe.wait_ge(acc_read, n + 1)
        turn_y(0, P)
        pe.wait_ge(y_copied, 2 * n + 1)
        turn_y(P, CAP2)

    @block.scalar
    def _(act):
        act.wait_ge(set_up, 1)
        squares = ps[:, 6:8, :].rearrange("p a b -> p (a b)")
        for tt in range(NT):
            act.drain()
            act.activation(squares, x_sb[:, tt, :], ACT.Square, accum_out=stat[:, tt:tt + 1])
        act.drain()
        act.activation(stat[:, 4:8], stat[:, 0:4], ACT.Sqrt, scale=1.0 / D, bias=eps).then_inc(rms, 1)
        for i in range(2 * NT):
            act.wait_ge(h_turned, i + 1)
            act.activation(hT[:, 4 * (i % 2):4 * (i % 2) + 4, (i // 2) * P:(i // 2 + 1) * P],
                           ps[:, i % 4, :].rearrange("p (a b) -> p a b", a=4), ACT.Copy).then_inc(hT_made, 1)
        act.wait_ge(gate_diff, 1)
        act.activation(gdiff[:, 4:8], gdiff[:, 0:4], ACT.Exp).then_inc(gate_exp, 1)
        act.wait_ge(passes_made, 1)
        n = n_passes(act)

        def copy_y(dst, rows):
            for h in range(2):
                ins = act.activation(dst[0:rows, 512 * h:512 * h + 512], ps[0:rows, 6 + h, :], ACT.Copy)
            ins.then_inc(y_copied, 1)

        with act.Fori(0, MAXPASS) as w:
            with act.If(w < n):
                for f in range(FT):
                    act.wait_ge(tile_done, w * FT + f + 1)
                    act.wait_ge(hid_made, w * FT + (f + FT - 1))
                    act.activation(silu_g[:, f % 2, :], ps[:, 3 + f % 3, 0:CAP], ACT.Silu).then_inc(silu_done, 1)
                    if f == 4:
                        act.wait_ge(y_turned, w * 2 + 1)
                        act.wait_ge(y_free, w + 1)
                        copy_y(y_rows, P)
                    if f == 6:
                        act.wait_ge(y_turned, w * 2 + 2)
                        copy_y(y_rows2, CAP2)
        act.wait_ge(y_turned, 2 * n + 1)
        act.wait_ge(y_free, n + 1)
        copy_y(y_rows, P)
        act.wait_ge(y_turned, 2 * n + 2)
        copy_y(y_rows2, CAP2)

    @block.gpsimd
    def _(pool):
        pool.memset(zero_i[:], 0)
        pool.memset(ones[:], 1.0)
        pool.memset(ones8, 1.0)
        pool.memset(eps, EPS)
        pool.memset(ident[:], 0.0)
        pool.iota(iota_e, [[1, 8]], base=0, channel_multiplier=0, allow_small_or_imprecise_dtypes=True)
        pool.iota(iota_w, [[1, 16]], base=0, channel_multiplier=0, allow_small_or_imprecise_dtypes=True)
        pool.iota(tok_i, [[P, NT]], base=0, channel_multiplier=1)
        pool.drain()
        pool.affine_select(ident[:], ident[:], [[-1, P]], ALU.not_equal, 1.0, base=0, channel_multiplier=1)
        pool.affine_select(t_lt[:], ones[:], [[1, P]], ALU.is_gt, 0.0, base=0, channel_multiplier=-1)
        pool.drain().then_inc(set_up, 1)
        rows = (MAXPASS + 1) * CAP
        zp = next(p for p in range(P, 0, -1) if rows % p == 0)
        pool.dma_start(slot_tok.rearrange("(p a) o -> p (a o)", p=zp), zero_i[0:zp, 0:rows // zp]).then_inc(table_zero, 16)
        pool.wait_ge(table_zero, 16)
        pool.wait_ge(slots_made, 1)
        for j in range(2 * NT):
            pool.indirect_dma_start(slot_tok, bass.IndirectOffsetOnAxis(ap=slot_i[:, j:j + 1], axis=0),
                                    tok_i[:, j % NT:j % NT + 1], None).then_inc(scattered, 16)
        pool.wait_ge(scattered, 16 * 2 * NT)
        pool.wait_ge(h_sent[0], 32)
        pool.wait_ge(h_sent[1], 32)

        def gather():
            pool.indirect_dma_start(x_rows[:], None, h_dram,
                                    bass.IndirectOffsetOnAxis(ap=idx_a, axis=0)).then_inc(rows_got, 16)
            pool.indirect_dma_start(x_rows2[0:CAP2, :], None, h_dram,
                                    bass.IndirectOffsetOnAxis(ap=idx_b[0:CAP2, :], axis=0)).then_inc(rows_got, 16)

        pool.dma_start(idx_a, slot_tok[0:P, :]).then_inc(idx_in, 16)
        pool.dma_start(idx_b[0:CAP2, :], slot_tok[P:CAP, :]).then_inc(idx_in, 16)
        pool.wait_ge(idx_in, 32)
        gather()
        pool.wait_ge(passes_made, 1)
        n = n_passes(pool)
        with pool.Fori(0, MAXPASS) as w:
            with pool.If(w < n):
                pool.wait_ge(x_turned, w * 2 + 2)
                pool.sem_inc(pool_step, 1)
                pool.dma_start(idx_a, slot_tok[bass.ds(w * CAP + CAP, P), :]).then_inc(idx_in, 16)
                pool.dma_start(idx_b[0:CAP2, :], slot_tok[bass.ds(w * CAP + CAP + P, CAP2), :]).then_inc(idx_in, 16)
                pool.wait_ge(idx_in, w * 32 + 64)
                pool.sem_inc(pool_step, 1)
                gather()
        pool.wait_ge(y_stored, 32 * n + 32)
        pool.sem_inc(pool_step, 1)
        for j in range(2 * NT):
            pool.indirect_dma_start(y_got[:, j, :], None, y_dram,
                                    bass.IndirectOffsetOnAxis(ap=slot_y[:, j:j + 1], axis=0)).then_inc(y_back[j], 16)

    @block.vector
    def _(dve):
        dve.memset(yT[:], 0.0)
        dve.wait_ge(rms, 1)
        dve.reciprocal(stat[:, 4:8], stat[:, 4:8])
        dve.drain()
        dve.wait_ge(moe_in, 32)
        for tt in range(NT):
            if tt >= 2:
                dve.wait_ge(h_sent[tt % 2], 16)
                dve.wait_ge(h_turned, 2 * tt - 2)
            dve.scalar_tensor_tensor(h_tok[:, tt % 2, :], x_sb[:, tt, :], stat[:, 4 + tt:5 + tt], gain[:],
                                     ALU.mult, ALU.mult).then_inc(h_made, 1)
        dve.wait_ge(routed, 1)
        dve.tensor_copy(logits, ps[:, 4, 0:32])
        dve.drain()
        for tt in range(NT):
            lg = logits[:, 8 * tt:8 * tt + 8]
            dve.max(tops[:, 8 * tt:8 * tt + 8], lg)
        dve.drain()
        for tt in range(NT):
            dve.max_index(top_i[:, tt, :], tops[:, 8 * tt:8 * tt + 8], logits[:, 8 * tt:8 * tt + 8])
        top3 = tops.rearrange("p (t k) -> p t k", t=NT)
        dve.tensor_tensor(gdiff[:, 0:4].unsqueeze(2), top3[:, :, 1:2], top3[:, :, 0:1], ALU.subtract
                          ).then_inc(gate_diff, 1)
        dve.drain()
        for k in range(2):
            dve.tensor_copy(chosen[:, 4 * k:4 * k + 4].unsqueeze(2), top_i[:, :, k:k + 1])
        dve.drain()
        dve.tensor_tensor(onehot.rearrange("p (j e) -> p j e", j=8), iota_e.unsqueeze(1).to_broadcast([P, 8, 8]),
                          chosen.unsqueeze(2).to_broadcast([P, 8, 8]), ALU.is_equal)
        dve.drain()
        dve.tensor_tensor(sel, onehot[:, 0:32], onehot[:, 32:64], ALU.add).then_inc(sel_made, 1)
        dve.wait_ge(gate_exp, 1)
        dve.tensor_scalar(gdiff[:, 8:12], gdiff[:, 4:8], 1.0, None, ALU.add)
        dve.drain()
        dve.reciprocal(gate[:, 0:4], gdiff[:, 8:12])
        dve.drain()
        dve.tensor_tensor(gate[:, 4:8], gate[:, 0:4], gdiff[:, 4:8], ALU.mult)
        dve.wait_ge(ranked, 1)
        dve.tensor_copy(rank, ps[:, 5, 0:32])
        dve.tensor_copy(cnt, ps[:, 5, 32:40])
        dve.drain()
        dve.tensor_scalar(nb, cnt, 0.0, None, ALU.is_gt)
        for k in range(1, (SEQ + CAP - 1) // CAP):
            dve.drain()
            dve.scalar_tensor_tensor(nb, cnt, float(CAP * k), nb, ALU.is_gt, ALU.add)
        dve.drain()
        dve.tensor_tensor_scan(end, ones8, nb, 0.0, ALU.mult, ALU.add)
        dve.drain()
        dve.tensor_tensor(first, end, nb, ALU.subtract)
        dve.drain()
        dve.tensor_scalar(first, first, float(CAP), None, ALU.mult)
        dve.drain()
        r3 = rank.rearrange("p (t e) -> p t e", t=NT)
        dve.tensor_tensor(r3, r3, first.unsqueeze(1).to_broadcast([P, NT, E]), ALU.add)
        dve.drain()
        dve.tensor_tensor(work.rearrange("p (k j) -> p k j", k=2), onehot.rearrange("p (k j) -> p k j", k=2),
                          rank.unsqueeze(1).to_broadcast([P, 2, 32]), ALU.mult)
        dve.drain()
        dve.reduce_sum(slot_f, work.rearrange("p (j e) -> p j e", j=8), AX.X)
        dve.drain()
        dve.tensor_copy(slot_i, slot_f)
        dve.tensor_scalar(slot_y, slot_f, float(CAP), None, ALU.add)
        dve.drain().then_inc(slots_made, 1)
        dve.tensor_copy(npass_i, end[:, 7:8])
        dve.tensor_scalar(pass_f, iota_w, end[:, 0:1], None, ALU.is_ge)
        for e in range(1, E - 1):
            dve.drain()
            dve.scalar_tensor_tensor(pass_f, iota_w, end[:, e:e + 1], pass_f, ALU.is_ge, ALU.add)
        dve.drain()
        dve.tensor_copy(pass_t[:], pass_f)
        dve.drain().then_inc(acc_read, 1)
        dve.drain().then_inc(passes_made, 1)
        dve.sem_inc(hid_made, FT)
        n = n_passes(dve)

        def copy_x_main():
            for h in range(2):
                ins = dve.tensor_copy(xT_next[:, 4 * h:4 * h + 4, 0:P], ps[:, 6 + h, :].rearrange("p (a b) -> p a b", a=4))
            ins.then_inc(x_copied, 1)

        def copy_x_rest():
            dve.tensor_copy(xT_next[:, :, P:CAP], ps[:, 6, 0:KD * CAP2].rearrange("p (a b) -> p a b", a=KD)
                            ).then_inc(x_copied, 1)

        dve.wait_ge(x_turned, 1)
        copy_x_main()
        dve.wait_ge(x_turned, 2)
        copy_x_rest()
        dve.drain()
        dve.tensor_copy(xT[:], xT_next[:]).then_inc(xT_made, 1)
        with dve.Fori(0, MAXPASS) as w:
            with dve.If(w < n):
                for f in range(FT):
                    dve.wait_ge(silu_done, w * FT + f + 1)
                    dve.tensor_tensor(hid[:, f, :], ps[:, 3 + f % 3, CAP:2 * CAP], silu_g[:, f % 2, :],
                                      ALU.mult).then_inc(hid_made, 1)
                    if f == 12:
                        dve.wait_ge(x_turned, w * 2 + 3)
                        copy_x_main()
                    if f == 16:
                        dve.wait_ge(x_turned, w * 2 + 4)
                        copy_x_rest()
                dve.drain()
                dve.tensor_copy(xT[:], xT_next[:]).then_inc(xT_made, 1)
                dve.wait_ge(down_done, w * ROUNDS + 2 * ROUNDS)
                for b in range(3):
                    m = min(3, KD - 3 * b)
                    dve.tensor_copy(yT[:, 3 * b:3 * b + m, :],
                                    ps[:, b, 0:m * CAP].rearrange("p (a b) -> p a b", a=m))
                dve.drain().then_inc(acc_read, 1)
        for tt in range(NT):
            for k in range(2):
                j = NT * k + tt
                dve.wait_ge(y_back[j], 16)
                dve.drain()
                ins = dve.scalar_tensor_tensor(x_sb[:, tt, :], y_got[:, j, :], gate[:, j:j + 1], x_sb[:, tt, :],
                                               ALU.mult, ALU.add)
            ins.then_inc(out_made, 1)

    block.__exit__(None, None, None)


INPUTS = ["x", "even_norm_mix", "even_w_in", "even_conv_w", "ssd_conv_w", "ssd_conv_b", "ssd_dt_bias", "ssd_a_log",
          "ssd_d", "ssd_norm_g", "even_w_out", "even_norm_ffn", "ffn_w_gate", "ffn_w_up", "ffn_w_down",
          "odd_norm_mix", "attn_w_qkv", "attn_q_norm", "attn_k_norm", "attn_lambda_q1", "attn_lambda_k1",
          "attn_lambda_q2", "attn_lambda_k2", "attn_sub_norm", "attn_w_o", "odd_norm_ffn",
          "moe_w_router", "moe_w_gate", "moe_w_up", "moe_w_down"]


def build(nc, t, out):
    y_dram = nc.dram_tensor("y_rows", ((MAXPASS + 1) * CAP, D), F32, kind="Internal").ap()
    r = build_trunk(nc, t, y_dram)
    build_experts(nc, t, out, r["place"], r["sem"], r["x_sb"], r["ps"], y_dram)


def rope_table():
    inv = (1.0 / (10000.0 ** (np.arange(0, HD, 2, dtype=np.float32) / HD))).astype(np.float32)
    ang = np.arange(SEQ, dtype=np.float32)[:, None] * inv[None, :]
    return np.stack([np.cos(ang), np.sin(ang)], axis=1).astype(np.float32)


def kernel(**inputs):
    from concourse import bacc
    from concourse.bass_utils import run_bass_kernel_spmd

    nc = bacc.Bacc("TRN2", target_bir_lowering=False, num_devices=1)
    arrays, t = {}, {}
    for name in INPUTS:
        a = np.ascontiguousarray(inputs[name])
        arrays[f"in_{name}"] = a
        t[name] = nc.dram_tensor(f"in_{name}", a.shape, mybir.dt.from_np(a.dtype), kind="ExternalInput").ap()
    arrays["in_rope"] = rope_table()
    t["rope"] = nc.dram_tensor("in_rope", (SEQ, 2, HD // 2), F32, kind="ExternalInput").ap()
    out = nc.dram_tensor("out_x", (1, SEQ, D), F32, kind="ExternalOutput").ap()
    build(nc, t, out)
    return run_bass_kernel_spmd(nc, [arrays], core_ids=[0]).results[0]["out_x"]
```

```python
import math

import numpy as np

import concourse.bass as bass
from concourse import mybir

F32 = mybir.dt.float32
F32R = mybir.dt.float32r
I32 = mybir.dt.int32
U32 = mybir.dt.uint32
ALU = mybir.AluOpType
ACT = mybir.ActivationFunctionType
AX = mybir.AxisListType

P = 128
D = 1024
SEQ = 512
NT = SEQ // P
KD = D // P
EPS = 1e-6

SSD_HEADS, SSD_HD, SSD_N = 16, 64, 64
GROUP_HEADS = SSD_HEADS // 2
XBC_TILES = (D + 4 * SSD_N) // P
COL_CG, COL_HV, COL_Z, COL_XBC = D, 2 * D, 3 * D, 4 * D
COL_END = 4 * D + XBC_TILES * P + SSD_HEADS

HEADS, HD = 16, 64
PAIRS = HEADS // 2
SCALE = 1.0 / math.sqrt(HD)
LAMBDA_INIT = 0.8 - 0.6 * math.exp(-0.3)
NEG = -1e30

FF = 2816
FT = FF // P
HALF_FT = FT // 2
HALF_UNITS = (HALF_FT + 1) // 2

E = 8
CAP = 160
MAXPASS = (2 * SEQ + E * (CAP - 1)) // CAP
ROUNDS = FT // 2
WSLOTS = 4
EARLY = WSLOTS - 1
WIDTHS = (112, 128, 136, 144, CAP)

RAW_SLOTS = 4
HL_SLOTS = 4
AHEAD = 3
UNIT = KD * P

U_XBC = 0
U_DT = U_XBC + XBC_TILES
U_Z = U_DT + 1
U_A = U_Z + 8
U_OUT = U_A + 3 * KD
U_FF = U_OUT + 16
FF_HALF = 2 * HALF_FT + 2 * HALF_UNITS
U_QKV = U_FF + 2 * FF_HALF
U_WO = U_QKV + 24
N_UNITS = U_WO + 8

G_Z, G_OUT, G_DOWN, G_QKV, G_WO = 0, 2, 4, 8, 14

R_CONV, R_SCONV, R_SBIAS = 0, 3 * KD, 3 * KD + 4 * XBC_TILES
N_ROWS = R_SBIAS + XBC_TILES


def build_trunk(nc, t, y_dram, h_slots):
    base = (nc.sbuf_base + 63) // 64 * 64
    top = nc.sbuf_usable_end

    def place(name, shape, dtype, offset):
        n = int(np.prod(shape[1:])) * 4
        assert base + offset + n <= top, (name, base + offset + n - top)
        return nc.alloc_sbuf_tensor_at(name, shape, dtype, offset=base + offset), offset + n

    K4 = 4096
    x_sb, o = place("x_sb", [P, NT, D], F32, 0)
    act_a_hi, o = place("act_a_hi", [P, KD, SEQ], F32R, o)
    act_a_lo, o_b = place("act_a_lo", [P, KD, SEQ], F32R, o)
    act_b_hi, o = place("act_b_hi", [P, KD, SEQ], F32R, o_b)
    act_b_lo, o = place("act_b_lo", [P, KD, SEQ], F32R, o)
    raw, o = place("raw", [P, RAW_SLOTS, UNIT], F32, o)
    w_hi, o = place("w_hi", [P, HL_SLOTS, UNIT], F32R, o)
    w_lo, o = place("w_lo", [P, HL_SLOTS, UNIT], F32R, o)
    gain, o = place("gain", [P, D], F32, o)
    htmp, o = place("htmp", [P, D], F32, o)
    ident, o = place("ident", [P, P], F32, o)
    t_incl, o = place("t_incl", [P, P], F32, o)
    t_gt, o = place("t_gt", [P, P], F32, o)
    ones, o = place("ones", [P, P], F32, o)
    cols, o = place("cols", [P, 80], F32, o)
    small, o = place("small", [P, 64], F32, o)
    stat, o = place("stat", [P, 64], F32, o)
    scratch = o

    xbcT, o = place("xbcT", [P, XBC_TILES, SEQ], F32, scratch)
    zs, o = place("zs", [P, NT, D], F32, o)
    xs, o = place("xs", [P, D], F32, o)
    b_tok, o = place("b_tok", [P, P], F32, o)
    xdt, o = place("xdt", [P, D], F32, o)
    xw, o = place("xw", [P, D], F32, o)
    dtri, o = place("dtri", [P, 4, P], F32, o)
    mix, o = place("mix", [P, SSD_HEADS, P], F32, o)
    cbm, o = place("cbm", [P, 2, P], F32, o)
    state, o = place("state", [P, 512], F32, o)
    es, o = place("es", [P, 48], F32, o)
    dts, o = place("dts", [P, 8, NT * SSD_HEADS], F32, o)
    o_conv = o
    conv_in, o = place("conv_in", [P, 520], F32, o_conv)
    conv_acc, cg_sb = htmp[:, 0:SEQ], htmp[:, SEQ:2 * SEQ]
    o_xs = scratch + XBC_TILES * SEQ * 4 + NT * D * 4
    xbc_in, o2 = place("xbc_in", [P, 2, 516], F32, o_xs)
    xbc_acc, o2 = place("xbc_acc", [P, 2, SEQ], F32, o2)
    dt_rows, o2 = place("dt_rows", [P, SEQ], F32, o2)
    rows_sb, o2 = place("rows_sb", [P, P], F32, o2)
    ff_hi, o = place("ff_hi", [P, HALF_FT, SEQ], F32R, scratch)
    ff_lo, o = place("ff_lo", [P, HALF_FT, SEQ], F32R, o)
    ff_gate, o = place("ff_gate", [P, 2, SEQ], F32, o)
    ff_val, o = place("ff_val", [P, 2, SEQ], F32, o)
    q_tok, o = place("q_tok", [P, NT, D], F32, scratch)
    k_tok, o = place("k_tok", [P, NT, D], F32, o)
    v_tok, o = place("v_tok", [P, NT, D], F32, o)
    trig, o = place("trig", [P, NT, 2, 32], F32, o)
    rot_c, o = place("rot_c", [P, 2, NT, HD], F32, o)
    rot_s, o = place("rot_s", [P, 2, NT, HD], F32, o)
    att_small, o = place("att_small", [P, 8 * HD], F32, o)
    head_ss, o = place("head_ss", [P, 64], F32, o)
    rot_tmp, o = place("rot_tmp", [P, SEQ], F32, o_b)
    rot_sum, o = place("rot_sum", [P, SEQ], F32, o)
    sq_tmp, o = place("sq_tmp", [P, SEQ], F32, o)
    qT, o = place("qT", [P, KD, SEQ], F32, SEQ * NT * 4 * 2)
    kT, o = place("kT", [P, KD, SEQ], F32, o)
    probs, o = place("probs", [P, 2, 2, SEQ], F32, scratch)
    diff, o = place("diff", [P, 2, SEQ], F32, o)
    diffT, o = place("diffT", [P, 2, SEQ], F32, o)
    soft, o3 = place("soft", [P, 2, 8], F32, scratch + 64 * 1024 // 1)
    o_tok, o = place("o_tok", [P, NT, D], F32, scratch + NT * D * 4)

    ps = nc.alloc_psum_tensor("ps", [P, 8, 512], F32)

    def flat(ap):
        return ap.bitcast(F32)

    sems = {}

    def sem(name):
        sems[name] = nc.alloc_semaphore(name)
        return sems[name]

    unit_in = [sem(f"unit_in{i}") for i in range(RAW_SLOTS)]
    hi_done, lo_done, unit_used = sem("hi_done"), sem("lo_done"), sem("unit_used")
    x_in, rows_in, small_in, gain_in = sem("x_in"), sem("rows_in"), sem("small_in"), sem("gain_in")
    att_in = sem("att_in")
    masks_ready, pads_ready = sem("masks_ready"), sem("pads_ready")
    zero_ready, y_zeroed = sem("zero_ready"), sem("y_zeroed")
    rows_turned, cols_ready = sem("rows_turned"), sem("cols_ready")
    sq_done, rms_done, h_ready = sem("sq_done"), sem("rms_done"), sem("h_ready")
    turned, hi_ev, lo_ev = sem("turned"), sem("hi_ev"), sem("lo_ev")
    xbc_evac, xbc_conv, xbc_silu = sem("xbc_evac"), sem("xbc_conv"), sem("xbc_silu")
    dt_evac, dt_turned, dt_abs, dt_exp, dt_ready = (sem("dt_evac"), sem("dt_turned"), sem("dt_abs"),
                                                    sem("dt_exp"), sem("dt_ready"))
    z_evac = sem("z_evac")
    cg_evac, cghv_ready, bg_used, ya_hi, ya_lo = (sem("cg_evac"), sem("cghv_ready"), sem("bg_used"),
                                                  sem("ya_hi"), sem("ya_lo"))
    xs_turned, ssd_small, seg_done = sem("xs_turned"), sem("ssd_small"), sem("seg_done")
    xs_evac, es_ready, seg_exp = sem("xs_evac"), sem("es_ready"), sem("seg_exp")
    dtri_ready, xdt_ready, xw_ready = sem("dtri_ready"), sem("xdt_ready"), sem("xw_ready")
    mix_ready, ssd_out, state_ready = sem("mix_ready"), sem("ssd_out"), sem("state_ready")
    dx_ready, y_evac, y_sq, y_rms = sem("dx_ready"), sem("y_evac"), sem("y_sq"), sem("y_rms")
    acc_evac, v_evac = sem("acc_evac"), sem("v_evac")
    ff_silu, ff_mul, ff_hi_done, ff_lo_done = sem("ff_silu"), sem("ff_mul"), sem("ff_hi_done"), sem("ff_lo_done")
    lam_exp, rot_tables, qk_sq, qk_rms, qk_ready = (sem("lam_exp"), sem("rot_tables"), sem("qk_sq"),
                                                    sem("qk_rms"), sem("qk_ready"))
    qk_root = sem("qk_root")
    qk_turned, qk_evac = sem("qk_turned"), sem("qk_evac")
    scores_done, bias_ready, exp_done, diff_ready = (sem("scores_done"), sem("bias_ready"),
                                                     sem("exp_done"), sem("diff_ready"))
    diff_turned, diffT_ready, heads_out, heads_evac = (sem("diff_turned"), sem("diffT_ready"),
                                                       sem("heads_out"), sem("heads_evac"))
    o_sq, o_rms = sem("o_sq"), sem("o_rms")

    def feature_unit(w, c):
        return w[:, c:c + P].rearrange("(k p) n -> p k n", p=P), (KD, P)

    def token_unit(w, k0, c, n=2):
        return w[k0 * P:(k0 + n) * P, c:c + 512].rearrange("(k p) n -> p k n", p=P), (n, 512)

    w_in, w_out = t["even_w_in"][0], t["even_w_out"][0]
    w_gate, w_up, w_down = t["ffn_w_gate"][0], t["ffn_w_up"][0], t["ffn_w_down"][0]
    w_qkv, w_o = t["attn_w_qkv"][0], t["attn_w_o"][0]
    units = [feature_unit(w_in, COL_XBC + P * f) for f in range(XBC_TILES)]
    units += [feature_unit(w_in, COL_END - P)]
    units += [token_unit(w_in, 2 * k, COL_Z + 512 * g) for g in range(2) for k in range(4)]
    units += [feature_unit(w_in, c + P * a) for a in range(KD) for c in (COL_CG, COL_HV, 0)]
    units += [token_unit(w_out, 2 * k, 512 * g) for g in range(2) for k in range(8)]
    for half in range(2):
        units += [feature_unit(w, P * f) for f in range(half * HALF_FT, (half + 1) * HALF_FT)
                  for w in (w_gate, w_up)]
        units += [token_unit(w_down, half * HALF_FT + 2 * k, 512 * g, min(2, HALF_FT - 2 * k))
                  for g in range(2) for k in range(HALF_UNITS)]
    units += [token_unit(w_qkv, 2 * k, 512 * g) for g in range(6) for k in range(4)]
    units += [token_unit(w_o, 2 * k, 512 * g) for g in range(2) for k in range(4)]
    assert len(units) == N_UNITS

    def size(u):
        return units[u][1][0] * units[u][1][1]

    gains = [t["even_norm_mix"], t["ssd_norm_g"], t["even_norm_ffn"], t["odd_norm_mix"], t["odd_norm_ffn"]]

    w_slots = []
    for s, at in enumerate((scratch, scratch + 24576, NT * D * 4, NT * D * 4 + 24576)):
        wg, o = place(f"w_gate{s}", [P, KD, 2 * P], F32, at)
        wu, o = place(f"w_up{s}", [P, KD, 2 * P], F32, o)
        wd, o = place(f"w_down{s}", [P, 2, D], F32, o)
        w_slots.append((wg, wu, wd))
    assert o <= NT * D * 4 * 4
    w_in = [sem(f"w_in{s}") for s in range(WSLOTS)]
    moe_in, set_up = sem("moe_in"), sem("set_up")
    w_router, o = place("w_router", [P, KD, E], F32, scratch + 57344)
    rt, o = place("rt", [P, 640], F32, o)
    idx, o = place("idx", [P, 32], I32, o)
    top_i, o = place("top_i", [P, NT, 8], U32, o)
    pass_t, o = place("pass_t", [P, 2, 16], I32, o)
    assert o <= scratch + 65536
    iota_e, iota_w = rt[:, 272:280], rt[:, 280:296]

    def load_expert_round(sp, e, r):
        wg, wu, wd = w_slots[r % WSLOTS]
        c = slice(2 * P * r, 2 * P * (r + 1))
        for dst, src in ((wg, t["moe_w_gate"][0][e, :, c]), (wu, t["moe_w_up"][0][e, :, c]),
                         (wd, t["moe_w_down"][0][e, c, :])):
            sp.dma_start(dst[:], src.rearrange("(k p) n -> p k n", p=P)).then_inc(w_in[r % WSLOTS], 16)

    block = nc.Block()
    block.__enter__()

    @block.sync
    def _(sp):
        rows = [(t["even_conv_w"][0].rearrange("j (f p) -> (j f) p", p=P), R_CONV, 3 * KD),
                (t["ssd_conv_w"][0].rearrange("j (f p) -> (j f) p", p=P), R_SCONV, 4 * XBC_TILES),
                (t["ssd_conv_b"].rearrange("o (f p) -> (o f) p", p=P), R_SBIAS, XBC_TILES)]
        sp.dma_start(x_sb[:], t["x"][0].rearrange("(t p) d -> p t d", p=P)).then_inc(x_in, 16)
        sp.dma_start(gain[:], gains[0][0].partition_broadcast(P)).then_inc(gain_in, 16)
        for src, r, n in rows:
            sp.dma_start(rows_sb[r:r + n, :], src).then_inc(rows_in, 16)
        for i, name in enumerate(("ssd_dt_bias", "ssd_a_log", "ssd_d")):
            sp.dma_start(small[:, 16 * i:16 * i + 16], t[name][0].partition_broadcast(P)).then_inc(small_in, 16)

        def load(u):
            src, (k, n) = units[u]
            if u >= RAW_SLOTS:
                sp.wait_ge(lo_done, u - RAW_SLOTS + 1)
            sp.dma_start(raw[:, u % RAW_SLOTS, 0:k * n].rearrange("p (k n) -> p k n", k=k),
                         src).then_inc(unit_in[u % RAW_SLOTS], 16)

        def load_gain(k):
            sp.wait_ge(h_ready, NT * k)
            sp.dma_start(gain[:], gains[k][0].partition_broadcast(P)).then_inc(gain_in, 16)

        for u in range(N_UNITS):
            load(u)
            if u == U_XBC + 6:
                sp.wait_ge(zero_ready, 1)
                for rows in (y_dram, h_slots):
                    for r in range(0, rows.shape[0], P):
                        m = min(P, rows.shape[0] - r)
                        sp.dma_start(rows[r:r + m, :], mix[0:m, 0:D // P, :].rearrange("p a b -> p (a b)")
                                     ).then_inc(y_zeroed, 16)
            if u == U_A:
                load_gain(1)
            if u == U_OUT + 8:
                load_gain(2)
            if u == U_FF + 8:
                load_gain(3)
            if u == U_FF + 2 * FF_HALF - 6:
                sp.wait_ge(ff_lo_done, FT)
                sp.dma_start(trig[:], t["rope"].rearrange("(t p) a c -> p t a c", p=P)).then_inc(att_in, 16)
                for i, name in enumerate(("attn_q_norm", "attn_k_norm", "attn_lambda_q1", "attn_lambda_k1",
                                          "attn_lambda_q2", "attn_lambda_k2")):
                    sp.dma_start(att_small[:, HD * i:HD * i + HD],
                                 t[name][0].partition_broadcast(P)).then_inc(att_in, 16)
                sp.dma_start(small[:, 63:64], t["attn_sub_norm"].rearrange("o d -> d o")).then_inc(att_in, 16)
                sp.dma_start(w_router[:], t["moe_w_router"][0].rearrange("(k p) e -> p k e", p=P)).then_inc(moe_in, 16)
        load_gain(4)
        sp.wait_ge(turned, 40)
        for r in range(EARLY):
            load_expert_round(sp, 0, r)

    @block.tensor
    def _(pe):
        def begin_unit(u):
            pe.wait_ge(lo_done, u + 1)

        def feature_out(u, bank, xh, xl):
            begin_unit(u)
            s = u % HL_SLOTS
            for k in range(KD):
                wh, wl = w_hi[:, s, k * P:(k + 1) * P], w_lo[:, s, k * P:(k + 1) * P]
                pe.matmul(ps[:, bank, :], wh, xh[:, k, :], start=(k == 0), stop=False)
                pe.matmul(ps[:, bank, :], wh, xl[:, k, :], start=False, stop=False)
                last = pe.matmul(ps[:, bank, :], wl, xh[:, k, :], start=False, stop=(k == KD - 1))
            last.then_inc(unit_used, 1)

        def token_out(g, u0, depth, source):
            b0 = 4 * (g % 2)
            for i in range((depth + 1) // 2):
                begin_unit(u0 + i)
                s = (u0 + i) % HL_SLOTS
                for tt in range(NT):
                    for k in range(2 * i, min(2 * i + 2, depth)):
                        xh, xl = source(k, tt)
                        c = (k - 2 * i) * 512
                        wh, wl = w_hi[:, s, c:c + 512], w_lo[:, s, c:c + 512]
                        pe.matmul(ps[:, b0 + tt, :], xh, wh, start=(k == 0), stop=False)
                        pe.matmul(ps[:, b0 + tt, :], xh, wl, start=False, stop=False)
                        last = pe.matmul(ps[:, b0 + tt, :], xl, wh, start=False, stop=(k == depth - 1))
                last.then_inc(unit_used, 1)

        def of(hi, lo, k0=0):
            return lambda k, tt: (hi[:, k - k0, tt * P:(tt + 1) * P], lo[:, k - k0, tt * P:(tt + 1) * P])

        def turn(n, source, first_bank):
            for tt in range(NT):
                pe.wait_ge(h_ready, NT * n + tt + 1)
                for half in range(2):
                    i = 8 * n + 2 * tt + half
                    bank = first_bank + (2 * tt + half) % 4
                    if 2 * tt + half >= 4:
                        pe.wait_ge(lo_ev, i - 3)
                    for j in range(4):
                        c = (4 * half + j) * P
                        mm = pe.transpose(ps[:, bank, j * P:(j + 1) * P], source(tt)[:, c:c + P], ident[:])
                    mm.then_inc(turned, 1)

        pe.wait_ge(masks_ready, 1)
        pe.wait_ge(rows_in, 48)
        pe.transpose(ps[:, 5, 0:N_ROWS], rows_sb[0:N_ROWS, :], ident[0:N_ROWS, 0:N_ROWS]).then_inc(rows_turned, 1)

        turn(0, lambda tt: htmp, 0)
        pe.wait_ge(lo_ev, 8)
        for f in range(XBC_TILES):
            if f >= 4:
                pe.wait_ge(xbc_evac, f - 3)
            feature_out(U_XBC + f, f % 4, act_a_hi, act_a_lo)
        feature_out(U_DT, 4, act_a_hi, act_a_lo)
        pe.wait_ge(dt_evac, 1)
        for tt in range(NT):
            mm = pe.transpose(ps[:, 5, tt * P:(tt + 1) * P], dt_rows[:, tt * P:(tt + 1) * P], ident[:])
        mm.then_inc(dt_turned, 1)
        pe.wait_ge(xbc_evac, XBC_TILES)
        token_out(G_Z, U_Z, KD, of(act_a_hi, act_a_lo))
        pe.wait_ge(dt_abs, 1)
        token_out(G_Z + 1, U_Z + 4, KD, of(act_a_hi, act_a_lo))

        def ssd_first(c):
            ts = slice(c * P, (c + 1) * P)
            if c >= 1:
                pe.wait_ge(y_evac, c)
                pe.wait_ge(state_ready, c)
            else:
                pe.wait_ge(xbc_silu, XBC_TILES)
                pe.wait_ge(z_evac, 2 * NT)
                pe.wait_ge(dt_ready, 1)
            for f in range(KD):
                pe.transpose(ps[:, 3 + f // 4, (f % 4) * P:(f % 4 + 1) * P], xbcT[:, f, ts], ident[:])
            pe.transpose(ps[:, 5, 0:P], xbcT[:, KD, ts], ident[:]).then_inc(xs_turned, 1)
            d = dts[:, 1, c * 16:c * 16 + 16]
            pe.matmul(ps[:, 5, 128:144], t_incl[:], d, start=True, stop=True)
            pe.matmul(ps[:, 5, 144:160], t_gt[:], d, start=True, stop=True)
            pe.matmul(ps[:, 5, 160:176], ones[:], d, start=True, stop=True)
            for g in range(2):
                r = slice(64 * g, 64 * g + 64)
                pe.drain()
                mm = pe.matmul(ps[:, 5, 192 + P * g:192 + P * g + P], xbcT[r, KD, ts], xbcT[r, KD + 1, ts],
                               start=True, stop=True)
            mm.then_inc(ssd_small, 1)
            for h in range(4):
                pe.wait_ge(dtri_ready, 4 * c + h + 1)
                if h >= 2:
                    pe.wait_ge(seg_exp, 4 * c + h - 1)
                pe.matmul(ps[:, 6 + h % 2, :], t_gt[:], dtri[:].rearrange("p a b -> p (a b)"),
                          start=True, stop=True).then_inc(seg_done, 1)

        def ssd_second(c):
            ts = slice(c * P, (c + 1) * P)
            pe.wait_ge(mix_ready, 4 * (c + 1))
            pe.wait_ge(xdt_ready, c + 1)
            pe.wait_ge(xw_ready, c + 1)
            pe.wait_ge(xs_evac, c + 1)
            for h in range(SSD_HEADS):
                q = h * SSD_HD
                pe.matmul(ps[:, 3 + h // 8, q % 512:q % 512 + SSD_HD], mix[:, h, :], xdt[:, q:q + SSD_HD],
                          start=True, stop=True)
            if c >= 1:
                for g in range(2):
                    r = slice(64 * g, 64 * g + 64)
                    mm = pe.matmul(ps[:, 6 + g, :], xbcT[r, KD + 1, ts], state[r, :], start=True, stop=True)
            if c < NT - 1:
                pe.wait_ge(es_ready, c + 1)
                for g in range(2):
                    r = slice(64 * g, 64 * g + 64)
                    mm = pe.matmul(ps[r, 5, :], b_tok[:, r], xw[:, 512 * g:512 * g + 512], start=True, stop=True)
            mm.then_inc(ssd_out, 1)

        for a in range(KD):
            if a == 0:
                pe.wait_ge(z_evac, 2 * NT)
            else:
                pe.wait_ge(cg_evac, a)
            feature_out(U_A + 3 * a, 0, act_a_hi, act_a_lo)
            if a >= 1:
                pe.wait_ge(cghv_ready, a)
            feature_out(U_A + 3 * a + 1, 1, act_a_hi, act_a_lo)
            if a >= 1:
                pe.wait_ge(bg_used, a)
            feature_out(U_A + 3 * a + 2, 2, act_a_hi, act_a_lo)
            (ssd_second if a % 2 else ssd_first)(a // 2)

        pe.wait_ge(bg_used, KD)
        pe.wait_ge(y_evac, NT)
        turn(1, lambda tt: zs[:, tt, :], 0)
        pe.wait_ge(ya_lo, KD)
        pe.wait_ge(lo_ev, 16)

        def mixed(k, tt):
            return of(act_b_hi, act_b_lo)(k, tt) if k < KD else of(act_a_hi, act_a_lo, KD)(k, tt)

        token_out(G_OUT, U_OUT, 2 * KD, mixed)
        token_out(G_OUT + 1, U_OUT + 8, 2 * KD, mixed)

        pe.wait_ge(acc_evac, 8)
        turn(2, lambda tt: htmp, 0)
        pe.wait_ge(lo_ev, 24)
        for half in range(2):
            u0 = U_FF + half * FF_HALF
            if half:
                pe.wait_ge(acc_evac, 12)
            for f in range(HALF_FT):
                n = half * HALF_FT + f
                if n >= 2:
                    pe.wait_ge(ff_mul, n - 1)
                feature_out(u0 + 2 * f, 2 * (n % 2), act_a_hi, act_a_lo)
                feature_out(u0 + 2 * f + 1, 2 * (n % 2) + 1, act_a_hi, act_a_lo)
            pe.wait_ge(ff_lo_done, HALF_FT * (half + 1))
            token_out(G_DOWN + 2 * half, u0 + 2 * HALF_FT, HALF_FT, of(ff_hi, ff_lo))
            if half:
                pe.wait_ge(acc_evac, 16)
            token_out(G_DOWN + 2 * half + 1, u0 + 2 * HALF_FT + HALF_UNITS, HALF_FT, of(ff_hi, ff_lo))

        pe.wait_ge(acc_evac, 24)
        turn(3, lambda tt: htmp, 0)
        pe.wait_ge(lo_ev, 32)
        for g in range(6):
            if g >= 2:
                pe.wait_ge(acc_evac, 24 + 4 * (g - 1))
            token_out(G_QKV + g, U_QKV + 4 * g, KD, of(act_a_hi, act_a_lo))
        pe.wait_ge(qk_ready, 16)
        pe.wait_ge(acc_evac, 40)
        pe.wait_ge(v_evac, 8)
        for i, source in enumerate((q_tok, k_tok)):
            for pair in range(PAIRS):
                n = 8 * i + pair
                if n >= 4:
                    pe.wait_ge(qk_evac, n - 3)
                for tt in range(NT):
                    mm = pe.transpose(ps[:, n % 4, tt * P:(tt + 1) * P],
                                      source[:, tt, pair * P:(pair + 1) * P], ident[:])
                mm.then_inc(qk_turned, 1)
        pe.wait_ge(qk_evac, 16)
        items = [(pair, i) for pair in range(PAIRS) for i in range(NT)]
        N = len(items)
        for n in range(N + 3):
            if n < N:
                pair, i = items[n]
                w = P * (i + 1)
                if n >= 2:
                    pe.wait_ge(exp_done, 2 * (n - 1))
                for m in range(2):
                    r = slice(64 * m, 64 * m + 64)
                    b = 2 * (n % 2) + m
                    pe.matmul(ps[:, b, 0:w], qT[r, pair, i * P:(i + 1) * P], kT[r, pair, 0:w],
                              start=True, stop=False, skip_group_check=True)
                    mm = pe.matmul(ps[:, b, w - 64:w], att_small[r, 0:P], att_small[r, P:P + 64],
                                   start=False, stop=True, skip_group_check=True)
                mm.then_inc(scores_done, 1)
            if 2 <= n < N + 2:
                pair, i = items[n - 2]
                pe.wait_ge(diff_ready, n - 1)
                if n >= 4:
                    pe.wait_ge(diffT_ready, n - 3)
                for b in range(i + 1):
                    mm = pe.transpose(ps[:, 4 + n % 2, b * P:(b + 1) * P],
                                      diff[:, n % 2, b * P:(b + 1) * P], ident[:])
                mm.then_inc(diff_turned, 1)
            if n >= 3:
                pair, i = items[n - 3]
                pe.wait_ge(diffT_ready, n - 2)
                if n >= 5:
                    pe.wait_ge(heads_evac, n - 4)
                for b in range(i + 1):
                    mm = pe.matmul(ps[:, 6 + (n - 3) % 2, 0:P], diffT[:, (n - 3) % 2, b * P:(b + 1) * P],
                                   v_tok[:, b, pair * P:(pair + 1) * P], start=(b == 0), stop=(b == i))
                mm.then_inc(heads_out, 1)
        turn(4, lambda tt: o_tok[:, tt, :], 0)
        pe.wait_ge(lo_ev, 40)
        token_out(G_WO, U_WO, KD, of(act_b_hi, act_b_lo))
        pe.wait_ge(heads_evac, N)
        token_out(G_WO + 1, U_WO + 4, KD, of(act_b_hi, act_b_lo))

    @block.scalar
    def _(act):
        made = [0]

        def high_parts(upto):
            while made[0] <= min(upto, N_UNITS - 1):
                u = made[0]
                act.wait_ge(unit_in[u % RAW_SLOTS], 16 * (u // RAW_SLOTS + 1))
                if u >= HL_SLOTS:
                    act.wait_ge(unit_used, u - HL_SLOTS + 1)
                act.activation(w_hi[:, u % HL_SLOTS, 0:size(u)], raw[:, u % RAW_SLOTS, 0:size(u)],
                               ACT.Copy).then_inc(hi_done, 1)
                made[0] += 1

        def after(u):
            high_parts(u + AHEAD)
            act.wait_ge(unit_used, u + 1)

        def sums_of_squares(k):
            for tt in range(NT):
                act.drain()
                act.activation(squares, x_sb[:, tt, :], ACT.Square,
                               accum_out=stat[:, 8 * k + tt:8 * k + tt + 1])
            act.drain()
            act.activation(stat[:, 8 * k + 4:8 * k + 8], stat[:, 8 * k:8 * k + 4], ACT.Sqrt,
                           scale=1.0 / D, bias=stat[:, 60:61]).then_inc(rms_done, 1)

        def turned_high(n, hi, first_bank, scale=1.0):
            for tt in range(NT):
                for half in range(2):
                    i = 8 * n + 2 * tt + half
                    act.wait_ge(turned, i + 1)
                    act.activation(hi[:, 4 * half:4 * half + 4, tt * P:(tt + 1) * P],
                                   ps[:, first_bank + (2 * tt + half) % 4, :].rearrange("p (a b) -> p a b", a=4),
                                   ACT.Copy, scale=scale).then_inc(hi_ev, 1)

        squares = ps[:, 6:8, :].rearrange("p a b -> p (a b)")

        act.wait_ge(x_in, 16)
        act.wait_ge(pads_ready, 1)
        sums_of_squares(0)
        high_parts(AHEAD)
        turned_high(0, act_a_hi, 0)
        for f in range(XBC_TILES + 1):
            if f < XBC_TILES:
                after(U_XBC + f)
                if f >= 2:
                    act.wait_ge(xbc_conv, f - 1)
                act.activation(xbc_in[:, f % 2, 3:515], ps[:, f % 4, :], ACT.Copy).then_inc(xbc_evac, 1)
            if f >= 1:
                act.wait_ge(xbc_conv, f)
                act.activation(xbcT[:, f - 1, :], xbc_acc[:, (f - 1) % 2, :], ACT.Silu).then_inc(xbc_silu, 1)
        after(U_DT)
        act.activation(dt_rows[:], ps[:, 4, :], ACT.Copy).then_inc(dt_evac, 1)
        for g in range(2):
            high_parts(U_Z + 4 * g + AHEAD)
            if g == 0:
                high_parts(U_Z + 4)
            after(U_Z + 4 * g + 3)
            for tt in range(NT):
                act.activation(zs[:, tt, 512 * g:512 * g + 512], ps[:, 4 * g + tt, :], ACT.Silu).then_inc(z_evac, 1)
        act.wait_ge(dt_abs, 1)
        act.activation(dts[:, 3, :], dts[:, 2, :], ACT.Exp, scale=-1.0)
        act.activation(small[:, 48:64], small[:, 16:32], ACT.Exp).then_inc(dt_exp, 1)

        def ssd_first(c):
            act.wait_ge(xs_turned, c + 1)
            if c >= 1:
                act.wait_ge(ssd_out, c)
                act.wait_ge(dx_ready, c)
            act.activation(xs[:, 0:512], ps[:, 3, :], ACT.Copy)
            act.activation(xs[:, 512:1024], ps[:, 4, :], ACT.Copy)
            act.wait_ge(ssd_small, c + 1)
            act.activation(b_tok[:], ps[:, 5, 0:P], ACT.Copy).then_inc(xs_evac, 1)
            if c >= 1:
                act.wait_ge(y_evac, c)
                act.wait_ge(state_ready, c)
            act.activation(es[:], ps[:, 5, 128:176], ACT.Exp).then_inc(es_ready, 1)
            if c == 0:
                act.wait_ge(y_zeroed, 32 * ((y_dram.shape[0] + P - 1) // P))
            for h in range(4):
                act.wait_ge(seg_done, 4 * c + h + 1)
                act.activation(mix[:, 4 * h:4 * h + 4, :], ps[:, 6 + h % 2, :].rearrange("p (a b) -> p a b", a=4),
                               ACT.Exp).then_inc(seg_exp, 1)

        def ssd_second(c):
            act.wait_ge(y_evac, c + 1)
            for g in range(2):
                act.activation(xw[:, 512 * g:512 * g + 512], zs[:, c, 512 * g:512 * g + 512], ACT.Square,
                               accum_out=stat[:, 40 + 2 * c + g:41 + 2 * c + g])
            act.drain().then_inc(y_sq, 1)

        for a in range(KD):
            after(U_A + 3 * a)
            if a >= 1:
                act.wait_ge(cghv_ready, a)
            act.activation(cg_sb, ps[:, 0, :], ACT.Copy).then_inc(cg_evac, 1)
            high_parts(U_A + 3 * a + 1 + AHEAD)
            after(U_A + 3 * a + 2)
            act.wait_ge(bg_used, a + 1)
            act.activation(act_b_hi[:, a, :], conv_acc, ACT.Copy).then_inc(ya_hi, 1)
            (ssd_second if a % 2 else ssd_first)(a // 2)
        act.drain()
        act.activation(stat[:, 48:56], stat[:, 40:48], ACT.Sqrt, scale=2.0 / D,
                       bias=stat[:, 60:61]).then_inc(y_rms, 1)
        turned_high(1, act_a_hi, 0)
        for g in range(2):
            for i in range(8):
                high_parts(U_OUT + 8 * g + i + AHEAD)
        act.wait_ge(acc_evac, 8)
        act.wait_ge(unit_used, U_FF)
        sums_of_squares(1)
        turned_high(2, act_a_hi, 0)
        for half in range(2):
            u0 = U_FF + half * FF_HALF
            for f in range(HALF_FT):
                n = half * HALF_FT + f
                after(u0 + 2 * f)
                if n >= 2:
                    act.wait_ge(ff_mul, n - 1)
                act.activation(ff_gate[:, n % 2, :], ps[:, 2 * (n % 2), :], ACT.Silu).then_inc(ff_silu, 1)
                high_parts(u0 + 2 * f + 1 + AHEAD)
                act.wait_ge(ff_mul, n + 1)
                if half and f == 0:
                    act.wait_ge(unit_used, u0)
                act.activation(ff_hi[:, f, :], ff_val[:, n % 2, :], ACT.Copy).then_inc(ff_hi_done, 1)
            for i in range(2 * HALF_UNITS):
                high_parts(u0 + 2 * HALF_FT + i + AHEAD)
        act.wait_ge(acc_evac, 24)
        sums_of_squares(2)
        turned_high(3, act_a_hi, 0)
        act.wait_ge(lam_exp, 1)
        act.activation(head_ss[:, 34:36], head_ss[:, 32:34], ACT.Exp).then_inc(lam_exp, 1)
        for g in range(6):
            for i in range(4):
                high_parts(U_QKV + 4 * g + i + AHEAD)
            act.wait_ge(unit_used, U_QKV + 4 * g + 4)
            if g < 4:
                for tt in range(NT):
                    n = 4 * g + tt
                    if n >= 1:
                        act.wait_ge(qk_rms, n)
                    act.activation(sq_tmp[:], ps[:, 4 * (g % 2) + tt, :], ACT.Square).then_inc(qk_sq, 1)
                    act.wait_ge(qk_rms, n + 1)
                    act.activation(head_ss[:, 8:16], head_ss[:, 0:8], ACT.Sqrt, scale=1.0 / HD,
                                   bias=stat[:, 60:61]).then_inc(qk_root, 1)
            else:
                for tt in range(NT):
                    act.activation(v_tok[:, tt, 512 * (g - 4):512 * (g - 4) + 512], ps[:, 4 * (g % 2) + tt, :],
                                   ACT.Copy).then_inc(v_evac, 1)
        for n in range(16):
            act.wait_ge(qk_turned, n + 1)
            act.activation((qT, kT)[n // 8][:, n % 8, :], ps[:, n % 4, :], ACT.Copy).then_inc(qk_evac, 1)
        items = [(pair, i) for pair in range(PAIRS) for i in range(NT)]
        N = len(items)
        for n in range(N + 3):
            if n < N:
                pair, i = items[n]
                w = P * (i + 1)
                act.wait_ge(bias_ready, n + 1)
                if n >= 2:
                    act.wait_ge(diff_ready, n - 1)
                for m in range(2):
                    act.activation(probs[:, n % 2, m, 0:w], ps[:, 2 * (n % 2) + m, 0:w], ACT.Exp, scale=SCALE,
                                   bias=soft[:, n % 2, m:m + 1], accum_out=soft[:, n % 2, 2 + m:3 + m])
                    act.drain().then_inc(exp_done, 1)
            if 2 <= n < N + 2:
                pair, i = items[n - 2]
                w = P * (i + 1)
                act.wait_ge(diff_turned, n - 1)
                if n >= 4:
                    act.wait_ge(heads_out, n - 3)
                act.activation(diffT[:, n % 2, 0:w], ps[:, 4 + n % 2, 0:w], ACT.Copy).then_inc(diffT_ready, 1)
            if n >= 3:
                pair, i = items[n - 3]
                act.wait_ge(heads_evac, n - 2)
                act.drain()
                act.activation(sq_tmp[:, 0:P], o_tok[:, i, pair * P:(pair + 1) * P], ACT.Square,
                               accum_out=head_ss[:, 8 * i + pair:8 * i + pair + 1])
        act.drain()
        act.activation(head_ss[:, 32:64], head_ss[:, 0:32], ACT.Sqrt, scale=1.0 / P,
                       bias=stat[:, 60:61]).then_inc(o_rms, 1)
        turned_high(4, act_b_hi, 0, small[:, 63:64])
        for i in range(8):
            high_parts(U_WO + i + AHEAD)

    @block.gpsimd
    def _(pool):
        made = [0]

        def low_parts(upto):
            while made[0] <= min(upto, N_UNITS - 1):
                u = made[0]
                pool.wait_ge(hi_done, u + 1)
                pool.tensor_tensor(w_lo[:, u % HL_SLOTS, 0:size(u)], raw[:, u % RAW_SLOTS, 0:size(u)],
                                   flat(w_hi[:, u % HL_SLOTS, 0:size(u)]), ALU.subtract).then_inc(lo_done, 1)
                made[0] += 1

        pool.memset(ones[:], 1.0)
        pool.memset(ident[:], 0.0)
        pool.drain()
        pool.affine_select(ident[:], ident[:], [[-1, P]], ALU.not_equal, 1.0, base=0, channel_multiplier=1)
        pool.affine_select(t_incl[:], ones[:], [[1, P]], ALU.is_ge, 0.0, base=0, channel_multiplier=-1)
        pool.affine_select(t_gt[:], ones[:], [[-1, P]], ALU.is_gt, 0.0, base=0, channel_multiplier=1)
        pool.drain().then_inc(masks_ready, 1)
        pool.memset(mix[:, 0:D // P, :], 0.0)
        pool.drain().then_inc(zero_ready, 1)
        low_parts(U_A + AHEAD - 1)

        def heads(ap, lo, n):
            return ap[:, lo:lo + n].unsqueeze(2).to_broadcast([P, n, SSD_HD])

        def ssd_first(c):
            d = dts[:, 1, c * 16:c * 16 + 16]
            for h in range(4):
                if 4 * c + h >= 1:
                    pool.wait_ge(seg_done, 4 * c + h)
                pool.tensor_tensor(dtri[:], t_incl[:].unsqueeze(1).to_broadcast([P, 4, P]),
                                   d[:, 4 * h:4 * h + 4].unsqueeze(2).to_broadcast([P, 4, P]),
                                   ALU.mult).then_inc(dtri_ready, 1)
            pool.wait_ge(xs_evac, c + 1)
            if c >= 1:
                pool.wait_ge(y_evac, c)
                pool.wait_ge(y_sq, c)
            v = xs[:].rearrange("p (h d) -> p h d", h=SSD_HEADS)
            pool.tensor_tensor(xdt[:].rearrange("p (h d) -> p h d", h=SSD_HEADS), v,
                               heads(dts[:, 0], c * 16, 16), ALU.mult).then_inc(xdt_ready, 1)
            pool.wait_ge(es_ready, c + 1)
            pool.drain()
            pool.tensor_tensor(xw[:].rearrange("p (h d) -> p h d", h=SSD_HEADS),
                               xdt[:].rearrange("p (h d) -> p h d", h=SSD_HEADS),
                               heads(es, 16, 16), ALU.mult).then_inc(xw_ready, 1)

        def ssd_second(c):
            pool.wait_ge(ssd_out, c + 1)
            pool.tensor_tensor(xw[:].rearrange("p (h d) -> p h d", h=SSD_HEADS),
                               xs[:].rearrange("p (h d) -> p h d", h=SSD_HEADS),
                               heads(small, 32, 16), ALU.mult).then_inc(dx_ready, 1)

        pool.wait_ge(small_in, 48)
        pool.wait_ge(dt_ready, 1)
        for a in range(KD):
            low_parts(U_A + 3 * a + 2 + AHEAD)
            pool.wait_ge(ya_hi, a + 1)
            pool.tensor_tensor(act_b_lo[:, a, :], conv_acc, flat(act_b_hi[:, a, :]),
                               ALU.subtract).then_inc(ya_lo, 1)
            (ssd_second if a % 2 else ssd_first)(a // 2)
        pool.iota(iota_e, [[1, 8]], base=0, channel_multiplier=0, allow_small_or_imprecise_dtypes=True)
        pool.iota(iota_w, [[1, 16]], base=0, channel_multiplier=0, allow_small_or_imprecise_dtypes=True)
        pool.drain().then_inc(set_up, 1)
        low_parts(U_FF + AHEAD - 1)
        for half in range(2):
            u0 = U_FF + half * FF_HALF
            for f in range(HALF_FT):
                n = half * HALF_FT + f
                low_parts(u0 + 2 * f + 1 + AHEAD)
                pool.wait_ge(ff_hi_done, n + 1)
                pool.tensor_tensor(ff_lo[:, f, :], ff_val[:, n % 2, :], flat(ff_hi[:, f, :]),
                                   ALU.subtract).then_inc(ff_lo_done, 1)
            low_parts(u0 + FF_HALF - 1 + AHEAD)
        low_parts(N_UNITS - 1)

    @block.vector
    def _(dve):
        def norm(k):
            dve.wait_ge(rms_done, (0, 1, 2)[k] + 1)
            n = (0, 2, 3)[k]
            dve.reciprocal(stat[:, 8 * k + 4:8 * k + 8], stat[:, 8 * k + 4:8 * k + 8])
            dve.drain()
            dve.wait_ge(gain_in, 16 * (n + 1))
            for tt in range(NT):
                if tt >= 1:
                    dve.wait_ge(turned, 8 * n + 2 * tt)
                dve.scalar_tensor_tensor(htmp[:], x_sb[:, tt, :], stat[:, 8 * k + 4 + tt:8 * k + 5 + tt],
                                         gain[:], ALU.mult, ALU.mult).then_inc(h_ready, 1)
                if tt >= 1:
                    turned_low(n, tt - 1, act_a_hi, act_a_lo)
            turned_low(n, NT - 1, act_a_hi, act_a_lo)

        def turned_low(n, tt, hi, lo, scale=1.0):
            for half in range(2):
                dve.wait_ge(hi_ev, 8 * n + 2 * tt + half + 1)
                dve.scalar_tensor_tensor(lo[:, 4 * half:4 * half + 4, tt * P:(tt + 1) * P],
                                         ps[:, (2 * tt + half) % 4, :].rearrange("p (a b) -> p a b", a=4), scale,
                                         flat(hi[:, 4 * half:4 * half + 4, tt * P:(tt + 1) * P]),
                                         ALU.mult, ALU.subtract).then_inc(lo_ev, 1)

        def col(r):
            return cols[:, r:r + 1]

        def add_to_x(g, last_unit, c0):
            dve.wait_ge(unit_used, last_unit + 1)
            for tt in range(NT):
                xx = x_sb[:, tt, c0:c0 + 512]
                dve.tensor_tensor(xx, ps[:, 4 * (g % 2) + tt, :], xx, ALU.add).then_inc(acc_evac, 1)

        dve.memset(stat[:, 60:61], EPS)
        dve.memset(xbc_in[:, :, 0:3], 0.0)
        dve.memset(conv_in[:, 0:2], 0.0)
        dve.drain().then_inc(pads_ready, 1)
        dve.wait_ge(rows_turned, 1)
        dve.tensor_copy(cols[:, 0:N_ROWS], ps[:, 5, 0:N_ROWS])
        norm(0)
        for f in range(XBC_TILES):
            w = [col(R_SCONV + XBC_TILES * j + f) for j in range(4)]
            src, acc = xbc_in[:, f % 2, :], xbc_acc[:, f % 2, :]
            dve.wait_ge(xbc_evac, f + 1)
            if f >= 2:
                dve.wait_ge(xbc_silu, f - 1)
            dve.tensor_scalar(acc, src[:, 0:512], w[0], col(R_SBIAS + f), ALU.mult, ALU.add)
            for j in range(1, 4):
                dve.drain()
                ins = dve.scalar_tensor_tensor(acc, src[:, j:j + 512], w[j], acc, ALU.mult, ALU.add)
            ins.then_inc(xbc_conv, 1)
        T16 = NT * SSD_HEADS
        dve.wait_ge(dt_turned, 1)
        dve.wait_ge(small_in, 48)
        v3 = dts[:, 0, :].rearrange("p (t h) -> p t h", t=NT)
        dve.tensor_tensor(v3, ps[:, 5, :].rearrange("p (t c) -> p t c", t=NT)[:, :, P - 16:P],
                          small[:, 0:16].unsqueeze(1).to_broadcast([P, NT, 16]), ALU.add)
        dve.drain()
        dve.scalar_tensor_tensor(dts[:, 2, :], dts[:, 0, :], -1.0, dts[:, 0, :], ALU.mult,
                                 ALU.max).then_inc(dt_abs, 1)
        dve.wait_ge(dt_exp, 1)
        u, r, q, s = dts[:, 3, :], dts[:, 4, :], dts[:, 5, :], dts[:, 6, :]
        dve.tensor_scalar(r, u, 2.0, None, ALU.add)
        dve.drain()
        dve.reciprocal(r, r)
        dve.drain()
        dve.tensor_tensor(r, r, u, ALU.mult)
        dve.drain()
        dve.tensor_tensor(q, r, r, ALU.mult)
        dve.drain()
        dve.tensor_scalar(s, q, 1.0 / 17, None, ALU.mult)
        for m in (15, 13, 11, 9, 7, 5, 3):
            dve.drain()
            dve.scalar_tensor_tensor(s, s, 1.0 / m, q, ALU.add, ALU.mult)
        dve.drain()
        dve.scalar_tensor_tensor(s, s, 1.0, r, ALU.add, ALU.mult)
        dve.drain()
        dve.tensor_scalar(s, s, 2.0, None, ALU.mult)
        dve.drain()
        dve.scalar_tensor_tensor(dts[:, 0, :], dts[:, 0, :], 0.0, s, ALU.max, ALU.add)
        dve.drain()
        dve.scalar_tensor_tensor(dts[:, 1, :].rearrange("p (t h) -> p t h", t=NT), v3, -1.0,
                                 small[:, 48:64].unsqueeze(1).to_broadcast([P, NT, 16]), ALU.mult,
                                 ALU.mult).then_inc(dt_ready, 1)

        def ssd_first(c):
            dve.wait_ge(es_ready, c + 1)
            for g in range(2):
                dve.tensor_tensor(cbm[:, g, :], ps[:, 5, 192 + P * g:192 + P * g + P], t_incl[:], ALU.mult)
            dve.drain()
            for h in range(4):
                dve.wait_ge(seg_exp, 4 * c + h + 1)
                m = mix[:, 4 * h:4 * h + 4, :]
                dve.tensor_tensor(m, m, cbm[:, h // 2, :].unsqueeze(1).to_broadcast([P, 4, P]),
                                  ALU.mult).then_inc(mix_ready, 1)

        def ssd_second(c):
            def grouped(ap):
                return ap.rearrange("p (h d) -> p h d", h=GROUP_HEADS)

            def spread(rows, lo):
                return es[rows, lo:lo + 8].unsqueeze(2).to_broadcast([rows.stop - rows.start, 8, SSD_HD])

            every = slice(0, P)
            dve.wait_ge(ssd_out, c + 1)
            if c >= 1:
                for g in range(2):
                    y = xdt[:, 512 * g:512 * g + 512]
                    dve.tensor_tensor(grouped(y), grouped(ps[:, 6 + g, :]), spread(every, 8 * g), ALU.mult)
            if c < NT - 1:
                if c == 0:
                    dve.tensor_copy(state[:], ps[:, 5, :]).then_inc(state_ready, 1)
                else:
                    for g in range(2):
                        r = slice(64 * g, 64 * g + 64)
                        dve.tensor_tensor(grouped(state[r, :]), grouped(state[r, :]), spread(r, 32 + 8 * g), ALU.mult)
                    dve.drain()
                    dve.tensor_tensor(state[:], ps[:, 5, :], state[:], ALU.add).then_inc(state_ready, 1)
            dve.wait_ge(dx_ready, c + 1)
            for g in range(2):
                dve.tensor_tensor(xw[:, 512 * g:512 * g + 512], ps[:, 3 + g, :], xw[:, 512 * g:512 * g + 512], ALU.add)
            dve.drain()
            if c >= 1:
                dve.tensor_tensor(xw[:], xw[:], xdt[:], ALU.add)
                dve.drain()
            dve.tensor_tensor(zs[:, c, :], zs[:, c, :], xw[:], ALU.mult).then_inc(y_evac, 1)

        for a in range(KD):
            w = [col(R_CONV + KD * j + a) for j in range(3)]
            dve.wait_ge(unit_used, U_A + 3 * a + 2)
            dve.wait_ge(cg_evac, a + 1)
            dve.tensor_tensor(conv_in[:, 2:514], ps[:, 1, :], cg_sb, ALU.mult).then_inc(cghv_ready, 1)
            if a >= 1:
                dve.wait_ge(ya_lo, a)
            dve.drain()
            dve.tensor_scalar(conv_acc, conv_in[:, 0:512], w[0], None, ALU.mult)
            for j in (1, 2):
                dve.drain()
                dve.scalar_tensor_tensor(conv_acc, conv_in[:, j:j + 512], w[j], conv_acc, ALU.mult, ALU.add)
            dve.wait_ge(unit_used, U_A + 3 * a + 3)
            dve.drain()
            dve.tensor_tensor(conv_acc, ps[:, 2, :], conv_acc, ALU.mult).then_inc(bg_used, 1)
            (ssd_second if a % 2 else ssd_first)(a // 2)
        dve.wait_ge(y_rms, 1)
        dve.wait_ge(gain_in, 32)
        dve.reciprocal(stat[:, 48:56], stat[:, 48:56])
        dve.drain()
        for c in range(NT):
            for g in range(2):
                z = zs[:, c, 512 * g:512 * g + 512]
                ins = dve.scalar_tensor_tensor(z, z, stat[:, 48 + 2 * c + g:49 + 2 * c + g],
                                               gain[:, 512 * g:512 * g + 512], ALU.mult, ALU.mult)
            ins.then_inc(h_ready, 1)
            if c >= 1:
                turned_low(1, c - 1, act_a_hi, act_a_lo)
        turned_low(1, NT - 1, act_a_hi, act_a_lo)
        add_to_x(G_OUT, U_OUT + 7, 0)
        add_to_x(G_OUT + 1, U_OUT + 15, 512)
        norm(1)
        for half in range(2):
            u0 = U_FF + half * FF_HALF
            for f in range(HALF_FT):
                n = half * HALF_FT + f
                dve.wait_ge(unit_used, u0 + 2 * f + 2)
                dve.wait_ge(ff_silu, n + 1)
                if n >= 2:
                    dve.wait_ge(ff_lo_done, n - 1)
                dve.tensor_tensor(ff_val[:, n % 2, :], ps[:, 2 * (n % 2) + 1, :], ff_gate[:, n % 2, :],
                                  ALU.mult).then_inc(ff_mul, 1)
            for g in range(2):
                add_to_x(G_DOWN + 2 * half + g, u0 + 2 * HALF_FT + (g + 1) * HALF_UNITS - 1, 512 * g)
        norm(2)
        dve.wait_ge(att_in, 128)
        for i in range(2):
            g1, g2 = att_small[:, HD * i:HD * i + 32], att_small[:, HD * i + 32:HD * i + 64]
            b1, b2 = (g.unsqueeze(1).to_broadcast([P, NT, 32]) for g in (g1, g2))
            cos, sin = trig[:, :, 0, :], trig[:, :, 1, :]
            dve.tensor_tensor(rot_c[:, i, :, 0:32], cos, b1, ALU.mult)
            dve.tensor_tensor(rot_c[:, i, :, 32:64], cos, b2, ALU.mult)
            dve.scalar_tensor_tensor(rot_s[:, i, :, 0:32], sin, -1.0, b2, ALU.mult, ALU.mult)
            dve.tensor_tensor(rot_s[:, i, :, 32:64], sin, b1, ALU.mult)
        for m in range(2):
            a1, a2 = (att_small[:, HD * (2 + 2 * m + j):HD * (3 + 2 * m + j)] for j in (0, 1))
            dve.tensor_tensor(a1, a1, a2, ALU.mult)
            dve.drain()
            dve.reduce_sum(head_ss[:, 32 + m:33 + m], a1, AX.X)
        dve.drain().then_inc(lam_exp, 1)
        dve.wait_ge(lam_exp, 2)
        dve.tensor_tensor(head_ss[:, 36:37], head_ss[:, 35:36], head_ss[:, 34:35], ALU.subtract)
        dve.drain()
        dve.tensor_scalar(stat[:, 61:62], head_ss[:, 36:37], -LAMBDA_INIT, None, ALU.add)
        dve.memset(att_small[:, 0:192], 0.0)
        dve.drain()
        for r in (0, 64):
            dve.memset(att_small[r:r + 1, 0:64], NEG)
            dve.memset(att_small[r:r + 1, 128:192], 1.0)
        for g in range(4):
            dst, i = (q_tok, k_tok)[g // 2], g // 2
            for tt in range(NT):
                n = 4 * g + tt
                bank = ps[:, 4 * (g % 2) + tt, :].rearrange("p (h d) -> p h d", h=8)
                c3 = rot_c[:, i, tt, :].unsqueeze(1).to_broadcast([P, 8, HD])
                s3 = rot_s[:, i, tt, :]
                tmp, tot = (b[:].rearrange("p (h d) -> p h d", h=8) for b in (rot_tmp, rot_sum))
                dve.wait_ge(qk_sq, n + 1)
                dve.reduce_sum(head_ss[:, 0:8], sq_tmp[:].rearrange("p (h d) -> p h d", h=8),
                               AX.X).then_inc(qk_rms, 1)
                dve.tensor_tensor(tot, bank, c3, ALU.mult)
                dve.tensor_tensor(tmp[:, :, 0:32], bank[:, :, 32:64],
                                  s3[:, 0:32].unsqueeze(1).to_broadcast([P, 8, 32]), ALU.mult)
                dve.tensor_tensor(tmp[:, :, 32:64], bank[:, :, 0:32],
                                  s3[:, 32:64].unsqueeze(1).to_broadcast([P, 8, 32]), ALU.mult).then_inc(acc_evac, 1)
                dve.drain()
                dve.tensor_tensor(tot, tot, tmp, ALU.add)
                dve.wait_ge(qk_root, n + 1)
                dve.reciprocal(head_ss[:, 16:24], head_ss[:, 8:16])
                dve.drain()
                dve.tensor_tensor(dst[:, tt, 512 * (g % 2):512 * (g % 2) + 512].rearrange("p (h d) -> p h d", h=8),
                                  tot, head_ss[:, 16:24].unsqueeze(2).to_broadcast([P, 8, HD]),
                                  ALU.mult).then_inc(qk_ready, 1)
                dve.drain()
        items = [(pair, i) for pair in range(PAIRS) for i in range(NT)]
        N = len(items)
        dve.wait_ge(qk_turned, 16)
        for n in range(N + 3):
            if n < N:
                pair, i = items[n]
                w = P * (i + 1)
                s2 = soft[:, n % 2, :]
                dve.wait_ge(scores_done, n + 1)
                for m in range(2):
                    dve.reduce_max(s2[:, 6 + m:7 + m], ps[:, 2 * (n % 2) + m, 0:w], AX.X)
                dve.drain()
                dve.tensor_scalar(s2[:, 0:2], s2[:, 6:8], -SCALE, None, ALU.mult).then_inc(bias_ready, 1)
            if n >= 3:
                pair, i = items[n - 3]
                dve.wait_ge(heads_out, n - 2)
                dve.tensor_copy(o_tok[:, i, pair * P:(pair + 1) * P],
                                ps[:, 6 + (n - 3) % 2, 0:P]).then_inc(heads_evac, 1)
            if 1 <= n <= N:
                pair, i = items[n - 1]
                w = P * (i + 1)
                b = (n - 1) % 2
                s2 = soft[:, b, :]
                dve.wait_ge(exp_done, 2 * n)
                dve.reciprocal(s2[:, 4:6], s2[:, 2:4])
                dve.drain()
                dve.tensor_scalar(s2[:, 5:6], s2[:, 5:6], stat[:, 61:62], None, ALU.mult)
                if n >= 3:
                    dve.wait_ge(diff_turned, n - 2)
                dve.tensor_scalar(diff[:, b, 0:w], probs[:, b, 0, 0:w], s2[:, 4:5], None, ALU.mult)
                dve.drain()
                dve.scalar_tensor_tensor(diff[:, b, 0:w], probs[:, b, 1, 0:w], s2[:, 5:6], diff[:, b, 0:w],
                                         ALU.mult, ALU.add).then_inc(diff_ready, 1)
        dve.tensor_scalar(small[:, 63:64], small[:, 63:64], 1.0 - LAMBDA_INIT, None, ALU.mult)
        dve.wait_ge(o_rms, 1)
        dve.reciprocal(head_ss[:, 32:64], head_ss[:, 32:64])
        dve.drain()
        for tt in range(NT):
            v = o_tok[:, tt, :].rearrange("p (h d) -> p h d", h=8)
            dve.tensor_tensor(v, v, head_ss[:, 32 + 8 * tt:40 + 8 * tt].unsqueeze(2).to_broadcast([P, 8, P]),
                              ALU.mult).then_inc(h_ready, 1)
            if tt >= 1:
                turned_low(4, tt - 1, act_b_hi, act_b_lo, small[:, 63:64])
        turned_low(4, NT - 1, act_b_hi, act_b_lo, small[:, 63:64])
        for g in range(2):
            add_to_x(G_WO + g, U_WO + 4 * g + 3, 512 * g)

    block.__exit__(None, None, None)
    return dict(x_sb=x_sb, sem=sem, place=place, ps=ps, gain=gain, gain_in=gain_in, ident=ident, ones=ones,
                t_incl=t_incl, stat=stat, w_slots=w_slots, w_in=w_in, moe_in=moe_in, w_router=w_router,
                rt=rt, idx=idx, top_i=top_i, pass_t=pass_t, load_expert_round=load_expert_round)


def build_experts(nc, out, y_dram, h_slots, x_sb, sem, place, ps, gain, gain_in, ident, ones, t_incl, stat,
                  w_slots, w_in, moe_in, w_router, rt, idx, top_i, pass_t, load_expert_round):
    CAP2 = CAP - P
    o = 4 * NT * D * 4
    hT, _ = place("hT", [P, KD, SEQ], F32, o)
    xT, o = place("xT", [P, KD, CAP], F32, o)
    xT_next, o = place("xT_next", [P, KD, CAP], F32, o)
    hid, o = place("hid", [P, FT, CAP], F32, o)
    silu_g, o = place("silu_g", [P, 2, CAP], F32, o)
    yT, o = place("yT", [P, KD, CAP], F32, o)
    x_rows, o = place("x_rows", [P, D], F32, o)
    x_rows2, o = place("x_rows2", [P, D], F32, o)
    y_rows, o = place("y_rows_sb", [P, D], F32, o)
    y_rows2, o = place("y_rows2_sb", [P, D], F32, o)
    h_tok, o = place("h_tok", [P, NT, D], F32, o)
    assert o <= 8 * NT * D * 4
    y_got, _ = place("y_got", [P, 2 * NT, D], F32, NT * D * 4)

    def cut(lo, n):
        return rt[:, lo:lo + n]

    ss, logits, tops = cut(0, 16), cut(16, 32), cut(48, 32)
    chosen, onehot = cut(80, 8), cut(96, 64)
    sel, rank, cnt = cut(160, 32), cut(192, 32), cut(224, 8)
    nb, end, first = cut(232, 8), cut(240, 8), cut(248, 8)
    slot_f, gate, iota_e, iota_w, ones8 = cut(256, 8), cut(264, 8), cut(272, 8), cut(280, 16), cut(296, 8)
    held, step_held = cut(304, 8), cut(312, 8)
    work, gdiff = cut(320, 64), cut(384, 12)
    pass_e, pass_n, pass_k = cut(400, 16), cut(416, 16), cut(432, 16)
    steps = cut(448, 128)
    slot_i, slot_y, npass_i = idx[:, 0:8], idx[:, 8:16], idx[:, 16:17]
    eps = stat[:, 60:61]

    rms, h_made = sem("moe_rms"), sem("h_made")
    h_turned, hT_made, routed = sem("h_turned"), sem("hT_made"), sem("routed")
    gate_diff, gate_exp, sel_made, ranked = sem("gate_diff"), sem("gate_exp"), sem("sel_made"), sem("ranked")
    slots_made, passes_made, scattered = sem("slots_made"), sem("passes_made"), sem("scattered")
    rows_got, pool_step = sem("rows_got"), sem("pool_step")
    x_turned, x_copied, xT_made = sem("x_turned"), sem("x_copied"), sem("xT_made")
    tile_done, silu_done, hid_made = sem("tile_done"), sem("silu_done"), sem("hid_made")
    down_done, acc_read = sem("down_done"), sem("acc_read")
    y_turned, y_copied, y_stored, y_free = sem("y_turned"), sem("y_copied"), sem("y_stored"), sem("y_free")
    y_back = [sem(f"y_back{i}") for i in range(2 * NT)]
    out_made, out_stored = sem("out_made"), sem("out_stored")

    def uses(s):
        return (ROUNDS - s + WSLOTS - 1) // WSLOTS

    def last_use(s):
        return s + WSLOTS * (uses(s) - 1)

    def n_passes(eng):
        return eng.value_load(npass_i[0:1, :], min_val=E, max_val=MAXPASS)

    block = nc.Block()
    block.__enter__()

    @block.sync
    def _(sp):
        sp.wait_ge(scattered, 16 * 2 * NT)
        sp.dma_start(x_rows[:], h_slots[0:P, :]).then_inc(rows_got, 16)
        sp.dma_start(x_rows2[0:CAP2, :], h_slots[P:CAP, :]).then_inc(rows_got, 16)
        sp.wait_ge(passes_made, 1)
        n = n_passes(sp)
        with sp.Fori(0, MAXPASS) as w:
            with sp.If(w < n):
                e = sp.value_load(pass_t[0:1, 0, bass.ds(w, 1)], min_val=0, max_val=E - 1)
                for r in range(EARLY, ROUNDS):
                    s = r % WSLOTS
                    free = r - WSLOTS + 1 + ROUNDS if r >= WSLOTS else last_use(s) + 1
                    sp.wait_ge(down_done, w * ROUNDS + free)
                    load_expert_round(sp, e, r)
                    if r == EARLY:
                        sp.wait_ge(x_turned, w * 2 + 2)
                        sp.dma_start(x_rows[:], h_slots[bass.ds(w * CAP + CAP, P), :]).then_inc(rows_got, 16)
                        sp.dma_start(x_rows2[0:CAP2, :], h_slots[bass.ds(w * CAP + CAP + P, CAP2), :]
                                     ).then_inc(rows_got, 16)
                    if r == 5:
                        sp.wait_ge(y_copied, w * 2 + 2)
                        sp.dma_start(y_dram[bass.ds(w * CAP, P), :], y_rows[:]).then_inc(y_stored, 16)
                        sp.dma_start(y_dram[bass.ds(w * CAP + P, CAP2), :], y_rows2[0:CAP2, :]).then_inc(y_stored, 16)
                    if r == 9:
                        sp.wait_ge(y_stored, w * 32 + 32)
                        sp.sem_inc(y_free, 1)
            with sp.If(w < n - 1):
                e = sp.value_load(pass_t[0:1, 0, bass.ds(w + 1, 1)], min_val=0, max_val=E - 1)
                for r in range(EARLY):
                    sp.wait_ge(down_done, w * ROUNDS + (ROUNDS + last_use(r) + 1))
                    load_expert_round(sp, e, r)
        sp.wait_ge(y_copied, 2 * n + 2)
        sp.dma_start(y_dram[bass.ds(n * CAP, P), :], y_rows[:]).then_inc(y_stored, 16)
        sp.dma_start(y_dram[bass.ds(n * CAP + P, CAP2), :], y_rows2[0:CAP2, :]).then_inc(y_stored, 16)
        for tt in range(NT):
            sp.wait_ge(out_made, tt + 1)
            sp.dma_start(out[0, tt * P:(tt + 1) * P, :], x_sb[:, tt, :]).then_inc(out_stored, 16)
        sp.wait_ge(out_stored, 16 * NT)

    @block.tensor
    def _(pe):
        pe.sem_inc(down_done, ROUNDS)
        pe.sem_inc(y_free, 1)
        for tt in range(NT):
            pe.wait_ge(h_made, tt + 1)
            for half in range(2):
                b = (2 * tt + half) % 4
                if 2 * tt + half >= 4:
                    pe.wait_ge(hT_made, 2 * tt + half - 3)
                for j in range(4):
                    c = (4 * half + j) * P
                    mm = pe.transpose(ps[:, b, j * P:(j + 1) * P], h_tok[:, tt, c:c + P], ident[:])
                mm.then_inc(h_turned, 1)
        pe.wait_ge(moe_in, 16)
        for tt in range(NT):
            pe.wait_ge(hT_made, 2 * tt + 2)
            for k in range(KD):
                mm = pe.matmul(ps[:, 4, 8 * tt:8 * tt + 8], hT[:, k, tt * P:(tt + 1) * P], w_router[:, k, :],
                               start=(k == 0), stop=(k == KD - 1))
        mm.then_inc(routed, 1)
        pe.wait_ge(sel_made, 1)
        for tt in range(NT):
            for u in range(tt + 1):
                pe.matmul(ps[:, 5, 8 * tt:8 * tt + 8], (t_incl if u == tt else ones)[:], sel[:, 8 * u:8 * u + 8],
                          start=(u == 0), stop=(u == tt))
        for u in range(NT):
            mm = pe.matmul(ps[:, 5, 32:40], ones[:], sel[:, 8 * u:8 * u + 8], start=(u == 0), stop=(u == NT - 1))
        mm.then_inc(ranked, 1)

        def turn_x_main():
            for k in range(KD):
                mm = pe.transpose(ps[:, 6 + k // 4, (k % 4) * P:(k % 4 + 1) * P], x_rows[:, k * P:(k + 1) * P], ident[:])
            mm.then_inc(x_turned, 1)

        def turn_x_rest():
            for k in range(KD):
                mm = pe.transpose(ps[:, 6, k * CAP2:(k + 1) * CAP2], x_rows2[0:CAP2, k * P:(k + 1) * P],
                                  ident[0:CAP2, 0:CAP2])
            mm.then_inc(x_turned, 1)

        def turn_y(lo, n):
            for k in range(KD):
                mm = pe.transpose(ps[0:n, 6 + k // 4, (k % 4) * P:(k % 4 + 1) * P], yT[:, k, lo:lo + n], ident[:])
            mm.then_inc(y_turned, 1)

        pe.wait_ge(rows_got, 32)
        turn_x_main()
        pe.wait_ge(x_copied, 1)
        turn_x_rest()
        pe.wait_ge(passes_made, 1)
        n = n_passes(pe)

        def one_pass(w, width):
            def hidden(f):
                s = (f // 2) % WSLOTS
                c = (f % 2) * P
                b = 3 + f % 3
                if f % 2 == 0:
                    pe.wait_ge(w_in[s], w * (48 * uses(s)) + 48 * (f // 2 // WSLOTS + 1))
                pe.wait_ge(hid_made, w * FT + (FT, FT - 2, FT - 1)[f] if f < 3 else w * FT + (FT + f - 2))
                for i in range(2):
                    for k in range(KD):
                        mm = pe.matmul(ps[:, b, i * CAP:i * CAP + width], w_slots[s][i][:, k, c:c + P],
                                       xT[:, k, 0:width], start=(k == 0), stop=(k == KD - 1))
                mm.then_inc(tile_done, 1)

            def down(r):
                pe.wait_ge(hid_made, w * FT + (FT + 2 * r + 2))
                for f in (2 * r, 2 * r + 1):
                    for d in range(KD):
                        mm = pe.matmul(ps[:, d // 3, (d % 3) * CAP:(d % 3) * CAP + width],
                                       w_slots[r % WSLOTS][2][:, f % 2, d * P:(d + 1) * P], hid[:, f, 0:width],
                                       start=(f == 0 and d % 3 == 0), stop=(f == FT - 1), skip_group_check=True)
                mm.then_inc(down_done, 1)

            pe.wait_ge(xT_made, w + 1)
            for r in range(ROUNDS):
                if r == 7:
                    pe.wait_ge(x_copied, w * 2 + 3)
                hidden(2 * r)
                hidden(2 * r + 1)
                if r == 1:
                    pe.wait_ge(acc_read, w + 1)
                    pe.wait_ge(x_copied, w * 2 + 2)
                    turn_y(0, P)
                if r == 2:
                    pe.wait_ge(y_copied, w * 2 + 1)
                    turn_y(P, CAP2)
                if r == 5:
                    pe.wait_ge(y_copied, w * 2 + 2)
                    pe.wait_ge(rows_got, w * 32 + 64)
                    turn_x_main()
                if r == 7:
                    turn_x_rest()
                if r >= 1:
                    down(r - 1)
            down(ROUNDS - 1)

        with pe.Fori(0, MAXPASS) as w:
            with pe.If(w < n):
                kind = pe.value_load(pass_t[0:1, 1, bass.ds(w, 1)], min_val=0, max_val=len(WIDTHS) - 1)
                for i, width in enumerate(WIDTHS):
                    with pe.If(kind == i):
                        one_pass(w, width)
        pe.wait_ge(acc_read, n + 1)
        turn_y(0, P)
        pe.wait_ge(y_copied, 2 * n + 1)
        turn_y(P, CAP2)

    @block.scalar
    def _(act):
        squares = ps[:, 6:8, :].rearrange("p a b -> p (a b)")
        for tt in range(NT):
            act.drain()
            act.activation(squares, x_sb[:, tt, :], ACT.Square, accum_out=ss[:, tt:tt + 1])
        act.drain()
        act.activation(ss[:, 4:8], ss[:, 0:4], ACT.Sqrt, scale=1.0 / D, bias=eps).then_inc(rms, 1)
        for i in range(2 * NT):
            act.wait_ge(h_turned, i + 1)
            act.activation(hT[:, 4 * (i % 2):4 * (i % 2) + 4, (i // 2) * P:(i // 2 + 1) * P],
                           ps[:, i % 4, :].rearrange("p (a b) -> p a b", a=4), ACT.Copy).then_inc(hT_made, 1)
        act.wait_ge(gate_diff, 1)
        act.activation(gdiff[:, 4:8], gdiff[:, 0:4], ACT.Exp).then_inc(gate_exp, 1)
        act.wait_ge(passes_made, 1)
        n = n_passes(act)

        def copy_y(dst, rows):
            for h in range(2):
                ins = act.activation(dst[0:rows, 512 * h:512 * h + 512], ps[0:rows, 6 + h, :], ACT.Copy)
            ins.then_inc(y_copied, 1)

        with act.Fori(0, MAXPASS) as w:
            with act.If(w < n):
                for f in range(FT):
                    act.wait_ge(tile_done, w * FT + f + 1)
                    act.wait_ge(hid_made, w * FT + (f + FT - 1))
                    act.activation(silu_g[:, f % 2, :], ps[:, 3 + f % 3, 0:CAP], ACT.Silu).then_inc(silu_done, 1)
                    if f == 4:
                        act.wait_ge(y_turned, w * 2 + 1)
                        act.wait_ge(y_free, w + 1)
                        copy_y(y_rows, P)
                    if f == 6:
                        act.wait_ge(y_turned, w * 2 + 2)
                        copy_y(y_rows2, CAP2)
        act.wait_ge(y_turned, 2 * n + 1)
        act.wait_ge(y_free, n + 1)
        copy_y(y_rows, P)
        act.wait_ge(y_turned, 2 * n + 2)
        copy_y(y_rows2, CAP2)

    @block.gpsimd
    def _(pool):
        pool.wait_ge(slots_made, 1)
        for j in range(2 * NT):
            pool.indirect_dma_start(h_slots, bass.IndirectOffsetOnAxis(ap=slot_i[:, j:j + 1], axis=0),
                                    h_tok[:, j % NT, :], None).then_inc(scattered, 16)
        pool.wait_ge(passes_made, 1)
        n = n_passes(pool)
        pool.wait_ge(y_stored, 32 * n + 32)
        pool.sem_inc(pool_step, 1)
        for j in range(2 * NT):
            pool.indirect_dma_start(y_got[:, j, :], None, y_dram,
                                    bass.IndirectOffsetOnAxis(ap=slot_y[:, j:j + 1], axis=0)).then_inc(y_back[j], 16)

    @block.vector
    def _(dve):
        dve.memset(yT[:], 0.0)
        dve.memset(ones8, 1.0)
        dve.wait_ge(rms, 1)
        dve.reciprocal(ss[:, 4:8], ss[:, 4:8])
        dve.drain()
        dve.wait_ge(gain_in, 80)
        for tt in range(NT):
            dve.scalar_tensor_tensor(h_tok[:, tt, :], x_sb[:, tt, :], ss[:, 4 + tt:5 + tt], gain[:],
                                     ALU.mult, ALU.mult).then_inc(h_made, 1)
        dve.wait_ge(routed, 1)
        dve.tensor_copy(logits, ps[:, 4, 0:32])
        dve.drain()
        for tt in range(NT):
            lg = logits[:, 8 * tt:8 * tt + 8]
            dve.max(tops[:, 8 * tt:8 * tt + 8], lg)
        dve.drain()
        for tt in range(NT):
            dve.max_index(top_i[:, tt, :], tops[:, 8 * tt:8 * tt + 8], logits[:, 8 * tt:8 * tt + 8])
        top3 = tops.rearrange("p (t k) -> p t k", t=NT)
        dve.tensor_tensor(gdiff[:, 0:4].unsqueeze(2), top3[:, :, 1:2], top3[:, :, 0:1], ALU.subtract
                          ).then_inc(gate_diff, 1)
        dve.drain()
        for k in range(2):
            dve.tensor_copy(chosen[:, 4 * k:4 * k + 4].unsqueeze(2), top_i[:, :, k:k + 1])
        dve.drain()
        dve.tensor_tensor(onehot.rearrange("p (j e) -> p j e", j=8), iota_e.unsqueeze(1).to_broadcast([P, 8, 8]),
                          chosen.unsqueeze(2).to_broadcast([P, 8, 8]), ALU.is_equal)
        dve.drain()
        dve.tensor_tensor(sel, onehot[:, 0:32], onehot[:, 32:64], ALU.add).then_inc(sel_made, 1)
        dve.wait_ge(gate_exp, 1)
        dve.tensor_scalar(gdiff[:, 8:12], gdiff[:, 4:8], 1.0, None, ALU.add)
        dve.drain()
        dve.reciprocal(gate[:, 0:4], gdiff[:, 8:12])
        dve.drain()
        dve.tensor_tensor(gate[:, 4:8], gate[:, 0:4], gdiff[:, 4:8], ALU.mult)
        dve.wait_ge(ranked, 1)
        dve.tensor_copy(rank, ps[:, 5, 0:32])
        dve.tensor_copy(cnt, ps[:, 5, 32:40])
        dve.memset(nb, 1.0)
        for k in range(1, (SEQ + CAP - 1) // CAP):
            dve.drain()
            dve.scalar_tensor_tensor(nb, cnt, float(CAP * k), nb, ALU.is_gt, ALU.add)
        dve.drain()
        dve.tensor_tensor_scan(end, ones8, nb, 0.0, ALU.mult, ALU.add)
        dve.drain()
        dve.tensor_tensor(first, end, nb, ALU.subtract)
        dve.drain()
        r3 = rank.rearrange("p (t e) -> p t e", t=NT)
        dve.scalar_tensor_tensor(r3, first.unsqueeze(1).to_broadcast([P, NT, E]), float(CAP), r3, ALU.mult, ALU.add)
        dve.drain()
        dve.tensor_tensor(work.rearrange("p (k j) -> p k j", k=2), onehot.rearrange("p (k j) -> p k j", k=2),
                          rank.unsqueeze(1).to_broadcast([P, 2, 32]), ALU.mult)
        dve.drain()
        dve.reduce_sum(slot_f, work.rearrange("p (j e) -> p j e", j=8), AX.X)
        dve.drain()
        dve.tensor_scalar(slot_i, slot_f, -1.0, None, ALU.add)
        dve.tensor_scalar(slot_y, slot_f, float(CAP - 1), None, ALU.add)
        dve.drain().then_inc(slots_made, 1)
        dve.tensor_copy(npass_i, end[:, 7:8])
        s3 = steps.rearrange("p (e w) -> p e w", e=8)
        for e in range(E):
            dve.tensor_scalar(s3[:, e, :], iota_w, end[:, e:e + 1], None, ALU.is_ge)
        dve.scalar_tensor_tensor(held, first, float(CAP), cnt, ALU.mult, ALU.add)
        dve.drain()
        dve.reduce_sum(pass_e, steps.rearrange("p (e w) -> p w e", e=8), AX.X)
        dve.tensor_tensor(step_held[:, 0:7], held[:, 1:8], held[:, 0:7], ALU.subtract)
        dve.drain()
        dve.tensor_scalar(pass_t[:, 0, :], pass_e, float(E - 1), None, ALU.min)
        dve.tensor_scalar(pass_n, iota_w, -float(CAP), held[:, 0:1], ALU.mult, ALU.add)
        for e in range(E - 1):
            dve.drain()
            dve.scalar_tensor_tensor(pass_n, s3[:, e, :], step_held[:, e:e + 1], pass_n, ALU.mult, ALU.add)
        dve.drain()
        dve.tensor_scalar(pass_k, pass_n, float(WIDTHS[0]), None, ALU.is_gt)
        for width in WIDTHS[1:-1]:
            dve.drain()
            dve.scalar_tensor_tensor(pass_k, pass_n, float(width), pass_k, ALU.is_gt, ALU.add)
        dve.drain()
        dve.tensor_copy(pass_t[:, 1, :], pass_k)
        dve.memset(ps[:, 0:6, :], 0.0)
        dve.drain().then_inc(acc_read, 1)
        dve.drain().then_inc(passes_made, 1)
        dve.sem_inc(hid_made, FT)
        n = n_passes(dve)

        def copy_x_main():
            for h in range(2):
                ins = dve.tensor_copy(xT_next[:, 4 * h:4 * h + 4, 0:P], ps[:, 6 + h, :].rearrange("p (a b) -> p a b", a=4))
            ins.then_inc(x_copied, 1)

        def copy_x_rest():
            dve.tensor_copy(xT_next[:, :, P:CAP], ps[:, 6, 0:KD * CAP2].rearrange("p (a b) -> p a b", a=KD)
                            ).then_inc(x_copied, 1)

        dve.wait_ge(x_turned, 1)
        copy_x_main()
        dve.wait_ge(x_turned, 2)
        copy_x_rest()
        dve.drain()
        dve.tensor_copy(xT[:], xT_next[:]).then_inc(xT_made, 1)
        with dve.Fori(0, MAXPASS) as w:
            with dve.If(w < n):
                for f in range(FT):
                    dve.wait_ge(silu_done, w * FT + f + 1)
                    dve.tensor_tensor(hid[:, f, :], ps[:, 3 + f % 3, CAP:2 * CAP], silu_g[:, f % 2, :],
                                      ALU.mult).then_inc(hid_made, 1)
                    if f == 12:
                        dve.wait_ge(x_turned, w * 2 + 3)
                        copy_x_main()
                    if f == 16:
                        dve.wait_ge(x_turned, w * 2 + 4)
                        copy_x_rest()
                dve.drain()
                dve.tensor_copy(xT[:], xT_next[:]).then_inc(xT_made, 1)
                dve.wait_ge(down_done, w * ROUNDS + 2 * ROUNDS)
                for b in range(3):
                    m = min(3, KD - 3 * b)
                    dve.tensor_copy(yT[:, 3 * b:3 * b + m, :],
                                    ps[:, b, 0:m * CAP].rearrange("p (a b) -> p a b", a=m))
                dve.drain().then_inc(acc_read, 1)
        for tt in range(NT):
            for k in range(2):
                j = NT * k + tt
                dve.wait_ge(y_back[j], 16)
                dve.drain()
                ins = dve.scalar_tensor_tensor(x_sb[:, tt, :], y_got[:, j, :], gate[:, j:j + 1], x_sb[:, tt, :],
                                               ALU.mult, ALU.add)
            ins.then_inc(out_made, 1)

    block.__exit__(None, None, None)


INPUTS = ["x", "even_norm_mix", "even_w_in", "even_conv_w", "ssd_conv_w", "ssd_conv_b", "ssd_dt_bias", "ssd_a_log",
          "ssd_d", "ssd_norm_g", "even_w_out", "even_norm_ffn", "ffn_w_gate", "ffn_w_up", "ffn_w_down",
          "odd_norm_mix", "attn_w_qkv", "attn_q_norm", "attn_k_norm", "attn_lambda_q1", "attn_lambda_k1",
          "attn_lambda_q2", "attn_lambda_k2", "attn_sub_norm", "attn_w_o", "odd_norm_ffn",
          "moe_w_router", "moe_w_gate", "moe_w_up", "moe_w_down"]


def build(nc, t, out):
    y_dram = nc.dram_tensor("y_rows", ((MAXPASS + 1) * CAP, D), F32, kind="Internal").ap()
    h_slots = nc.dram_tensor("h_slots", ((MAXPASS + 1) * CAP, D), F32, kind="Internal").ap()
    build_experts(nc, out, y_dram, h_slots, **build_trunk(nc, t, y_dram, h_slots))


def rope_table():
    inv = (1.0 / (10000.0 ** (np.arange(0, HD, 2, dtype=np.float32) / HD))).astype(np.float32)
    ang = np.arange(SEQ, dtype=np.float32)[:, None] * inv[None, :]
    return np.stack([np.cos(ang), np.sin(ang)], axis=1).astype(np.float32)


def kernel(**inputs):
    from concourse import bacc
    from concourse.bass_utils import run_bass_kernel_spmd

    nc = bacc.Bacc("TRN2", target_bir_lowering=False, num_devices=1)
    arrays, t = {}, {}
    for name in INPUTS:
        a = np.ascontiguousarray(inputs[name])
        arrays[f"in_{name}"] = a
        t[name] = nc.dram_tensor(f"in_{name}", a.shape, mybir.dt.from_np(a.dtype), kind="ExternalInput").ap()
    arrays["in_rope"] = rope_table()
    t["rope"] = nc.dram_tensor("in_rope", (SEQ, 2, HD // 2), F32, kind="ExternalInput").ap()
    out = nc.dram_tensor("out_x", (1, SEQ, D), F32, kind="ExternalOutput").ap()
    build(nc, t, out)
    return run_bass_kernel_spmd(nc, [arrays], core_ids=[0]).results[0]["out_x"]
```
